# Optimizing a Trainium2 kernel written in Bass

```python
import math
import jax
import jax.numpy as jnp
from jax import lax
import numpy as np

D_MODEL = 1024
BATCH = 1
SEQ = 128
DEPTH = 2
DEC_BATCH = 1
DEC_SEQ = 512
PAST_LEN = 128

GRID_W = 64
N_BRANCH = 3
BRANCH_W = D_MODEL // 2
HY_ORDER = 2
HY_WIDTH = BRANCH_W
HY_POS_BANDS = 16
HY_POS_DIM = 1 + 2 * HY_POS_BANDS
HY_FILT_HIDDEN = 64
HY_DECAY_TARGET = 1e-2
HY_FAST_DECAY = 0.3
HY_SLOW_DECAY = 1.5
NA_HEADS = 8
NA_HEAD_DIM = BRANCH_W // NA_HEADS
NA_WIN_ROWS = 8
NA_WIN_COLS = 16
DA_HEADS = 8
DA_HEAD_DIM = BRANCH_W // (2 * DA_HEADS)
DA_V_DIM = 2 * DA_HEAD_DIM
D_FF = -(-(8 * D_MODEL) // (3 * 256)) * 256
IN_W = 3 * HY_WIDTH + 3 * BRANCH_W + 3 * BRANCH_W + N_BRANCH * D_MODEL
ROPE_BASE = 10000.0
EPS = 1e-6
Q_BLOCK = 128
NEG_INF = -1e30

kernel_name = 'hybrid_diffusion_trunk_step'

def rmsnorm(x, g):
    xf = x.astype(jnp.float32)
    y = xf * lax.rsqrt(jnp.mean(jnp.square(xf), axis=-1, keepdims=True) + EPS)
    return (y * g.astype(jnp.float32)).astype(x.dtype)

def modulated_norm(x, g, shift, scale):
    return rmsnorm(x, g) * (1 + scale[:, None, :]) + shift[:, None, :]

def short_conv(u, w, b):
    up = jnp.pad(u, ((0, 0), (1, 1), (0, 0)))
    return up[:, :-2] * w[0] + up[:, 1:-1] * w[1] + up[:, 2:] * w[2] + b

def hyena_filters(L, w1, b1, w2, b2, w3, freq):
    f32 = jnp.float32
    pos = jnp.arange(L, dtype=f32)
    t = pos / L
    bands = jnp.linspace(1e-4, HY_POS_BANDS - 1, HY_POS_BANDS, dtype=f32)
    ang = (2 * math.pi / L) * pos[:, None] * bands[None, :]
    feats = jnp.concatenate([t[:, None], jnp.cos(ang), -jnp.sin(ang)], axis=-1)
    fr = freq.astype(f32)
    h = jnp.sin(fr * (feats @ w1.astype(f32) + b1.astype(f32)))
    h = jnp.sin(fr * (h @ w2.astype(f32) + b2.astype(f32)))
    h = (h @ w3.astype(f32)).reshape(L, HY_ORDER, 2, HY_WIDTH)
    deltas = jnp.linspace(math.log(HY_DECAY_TARGET) / HY_SLOW_DECAY,
                          math.log(HY_DECAY_TARGET) / HY_FAST_DECAY, HY_WIDTH, dtype=f32)
    decay = jnp.exp(-t[:, None] * jnp.abs(deltas)[None, :])
    h = h * decay[:, None, None, :]
    h_fwd, h_bwd = h[:, :, 0], h[:, :, 1]
    h_full = jnp.concatenate([h_fwd, jnp.zeros((1, HY_ORDER, HY_WIDTH), f32), h_bwd[1:][::-1]], axis=0)
    h_full = h_full / jnp.sum(jnp.abs(h_full), axis=0, keepdims=True)
    return jnp.fft.rfft(h_full, n=2 * L, axis=0)

def long_conv(z, h_freq, bias):
    L = z.shape[1]
    zf = z.astype(jnp.float32)
    y = jnp.fft.irfft(jnp.fft.rfft(zf, n=2 * L, axis=1) * h_freq[None], n=2 * L, axis=1)[:, :L]
    return (y + zf * bias.astype(jnp.float32)).astype(z.dtype)

def hyena_mixer(u, conv_w, conv_b, fw1, fb1, fw2, fb2, fw3, ffreq, fbias):
    L = u.shape[1]
    v, x1, x2 = jnp.split(short_conv(u, conv_w, conv_b), 3, axis=-1)
    hf = hyena_filters(L, fw1, fb1, fw2, fb2, fw3, ffreq)
    z = x1 * long_conv(v, hf[:, 0], fbias[0])
    z = x2 * long_conv(z, hf[:, 1], fbias[1])
    return z

def map_query_blocks(fn, q):
    B, L = q.shape[:2]
    nb = L // Q_BLOCK
    qb = jnp.swapaxes(q, 0, 1).reshape((nb, Q_BLOCK, B) + q.shape[2:])
    out = lax.map(fn, qb)
    out = out.reshape((L, B) + out.shape[3:])
    return jnp.swapaxes(out, 0, 1)

def context_attention(q, k, v):
    B, L, H, dh = q.shape
    scale = dh ** -0.5

    def block(qb):
        s = jnp.einsum('qbhd,bkhd->bhqk', qb, k).astype(jnp.float32) * scale
        p = jax.nn.softmax(s, axis=-1).astype(v.dtype)
        return jnp.einsum('bhqk,bkhd->qbhd', p, v)

    return map_query_blocks(block, q).reshape(B, L, H * dh)

def neighbourhood_attention(q, k, v, k_ctx, v_ctx, rpb):
    B, L, H, dh = q.shape
    rows = L // GRID_W
    wr = min(NA_WIN_ROWS, rows)
    scale = dh ** -0.5
    r = jnp.arange(rows)
    r0 = jnp.clip(r - wr // 2, 0, rows - wr)
    row_idx = r0[:, None] + jnp.arange(wr)[None, :]
    c = jnp.arange(GRID_W)
    c0 = jnp.clip(c - NA_WIN_COLS // 2, 0, GRID_W - NA_WIN_COLS)
    col_ok = (c[None, :] >= c0[:, None]) & (c[None, :] < c0[:, None] + NA_WIN_COLS)
    dr = row_idx - r[:, None]
    dc = jnp.clip(c[None, :] - c[:, None], -(NA_WIN_COLS - 1), NA_WIN_COLS - 1)
    bias = rpb[:, dr[:, None, :, None] + NA_WIN_ROWS - 1, dc[None, :, None, :] + NA_WIN_COLS - 1]
    qg = q.reshape(B, rows, GRID_W, H, dh)
    kg = k.reshape(B, rows, GRID_W, H, dh)[:, row_idx]
    vg = v.reshape(B, rows, GRID_W, H, dh)[:, row_idx]
    s_lat = jnp.einsum('brqhd,brwkhd->bhrqwk', qg, kg).astype(jnp.float32) * scale + bias.astype(jnp.float32)[None]
    s_lat = jnp.where(col_ok[None, None, None, :, None, :], s_lat, NEG_INF)
    s_ctx = jnp.einsum('brqhd,bkhd->bhrqk', qg, k_ctx).astype(jnp.float32) * scale
    n_lat = wr * GRID_W
    s = jnp.concatenate([s_lat.reshape(B, H, rows, GRID_W, n_lat), s_ctx], axis=-1)
    p = jax.nn.softmax(s, axis=-1).astype(v.dtype)
    p_lat = p[..., :n_lat].reshape(B, H, rows, GRID_W, wr, GRID_W)
    p_ctx = p[..., n_lat:]
    o = jnp.einsum('bhrqwk,brwkhd->brqhd', p_lat, vg) + jnp.einsum('bhrqk,bkhd->brqhd', p_ctx, v_ctx)
    return o.reshape(B, L, H * dh)

def axial_rope(x):
    L = x.shape[1]
    f32 = jnp.float32
    pos = jnp.arange(L)
    row = (pos // GRID_W).astype(f32)
    col = (pos % GRID_W).astype(f32)
    n_freq = DA_HEAD_DIM // 4
    inv = ROPE_BASE ** (-jnp.arange(n_freq, dtype=f32) / n_freq)
    ang = jnp.concatenate([row[:, None] * inv[None, :], col[:, None] * inv[None, :]], axis=-1)
    cos = jnp.cos(ang)[None, :, None, None, :]
    sin = jnp.sin(ang)[None, :, None, None, :]
    xp = x.astype(f32).reshape(x.shape[:-1] + (DA_HEAD_DIM // 2, 2))
    x0, x1 = xp[..., 0], xp[..., 1]
    out = jnp.stack([x0 * cos - x1 * sin, x0 * sin + x1 * cos], axis=-1).reshape(x.shape)
    return out.astype(x.dtype)

def diff_attention(q, k, v, lam, lam_init, subln):
    B, L, H = q.shape[:3]
    scale = DA_HEAD_DIM ** -0.5

    def block(qb):
        s = jnp.einsum('qbhid,bkhid->bhiqk', qb, k).astype(jnp.float32) * scale
        p = jax.nn.softmax(s, axis=-1)
        a = (p[:, :, 0] - lam * p[:, :, 1]).astype(v.dtype)
        return jnp.einsum('bhqk,bkhd->qbhd', a, v)

    o = map_query_blocks(block, q)
    o = rmsnorm(o, subln) * (1 - lam_init)
    return o.reshape(B, L, H * DA_V_DIM)

def trunk_layer(x, mod, ctx_cache, lam_init, norm_mix, norm_ffn, w_in, hy_conv_w, hy_conv_b,
                hy_filt_w1, hy_filt_b1, hy_filt_w2, hy_filt_b2, hy_filt_w3, hy_filt_freq, hy_bias,
                na_rpb, da_lambda, da_subln, w_lift, w_out, w_ffn_in, w_ffn_out):
    B, L, _ = x.shape
    shift1, scale1, gate1, shift2, scale2, gate2 = jnp.split(mod, 6, axis=-1)
    h = modulated_norm(x, norm_mix, shift1, scale1)
    u = h @ w_in
    u_hy, u_na, u_da, u_gate = jnp.split(
        u, [3 * HY_WIDTH, 3 * HY_WIDTH + 3 * BRANCH_W, 3 * HY_WIDTH + 6 * BRANCH_W], axis=-1)
    y_hy = hyena_mixer(u_hy, hy_conv_w, hy_conv_b, hy_filt_w1, hy_filt_b1, hy_filt_w2, hy_filt_b2,
                       hy_filt_w3, hy_filt_freq, hy_bias)
    na_q, na_k, na_v = [t.reshape(B, L, NA_HEADS, NA_HEAD_DIM) for t in jnp.split(u_na, 3, axis=-1)]
    da_q, da_k, da_v = jnp.split(u_da, 3, axis=-1)
    da_q = da_q.reshape(B, L, DA_HEADS, 2, DA_HEAD_DIM)
    da_k = da_k.reshape(B, L, DA_HEADS, 2, DA_HEAD_DIM)
    da_v = da_v.reshape(B, L, DA_HEADS, DA_V_DIM)
    lam_p = da_lambda.astype(jnp.float32)
    lam = jnp.exp(jnp.sum(lam_p[0] * lam_p[1])) - jnp.exp(jnp.sum(lam_p[2] * lam_p[3])) + lam_init
    if ctx_cache is None:
        y_na = context_attention(na_q, na_k, na_v)
        y_da = diff_attention(da_q, da_k, da_v, lam, lam_init, da_subln)
        ctx_out = (na_k, na_v, da_k.reshape(B, L, DA_HEADS, 2 * DA_HEAD_DIM), da_v)
    else:
        na_k_ctx, na_v_ctx, da_k_ctx, da_v_ctx = ctx_cache
        Lc = da_k_ctx.shape[1]
        y_na = neighbourhood_attention(na_q, na_k, na_v, na_k_ctx, na_v_ctx, na_rpb)
        k_all = jnp.concatenate([axial_rope(da_k), da_k_ctx.reshape(B, Lc, DA_HEADS, 2, DA_HEAD_DIM)], axis=1)
        v_all = jnp.concatenate([da_v, da_v_ctx], axis=1)
        y_da = diff_attention(axial_rope(da_q), k_all, v_all, lam, lam_init, da_subln)
        ctx_out = None
    g = jax.nn.sigmoid(u_gate).reshape(B, L, N_BRANCH, D_MODEL)
    merged = (g[:, :, 0] * (y_hy @ w_lift[0]) + g[:, :, 1] * (y_na @ w_lift[1])
              + g[:, :, 2] * (y_da @ w_lift[2]))
    x = x + gate1[:, None, :] * (merged @ w_out)
    h2 = modulated_norm(x, norm_ffn, shift2, scale2)
    f_gate, f_up = jnp.split(h2 @ w_ffn_in, 2, axis=-1)
    x = x + gate2[:, None, :] * ((jax.nn.silu(f_gate) * f_up) @ w_ffn_out)
    return x, ctx_out

def setup_inputs(seed: int = 0) -> dict:
    key = jax.random.key(seed)
    ks = jax.random.split(key, 32)

    def nrm(k, shape, scale):
        return jax.random.normal(k, shape, jnp.float32) * scale

    return {
        'x_prompt': nrm(ks[0], (BATCH, SEQ, D_MODEL), 1.0),
        'x_sample': nrm(ks[1], (DEC_BATCH, DEC_SEQ, D_MODEL), 1.0),
        'cache_na_k': nrm(ks[2], (DEC_BATCH, DEPTH, PAST_LEN, NA_HEADS, NA_HEAD_DIM), 1.0),
        'cache_na_v': nrm(ks[3], (DEC_BATCH, DEPTH, PAST_LEN, NA_HEADS, NA_HEAD_DIM), 1.0),
        'cache_da_k': nrm(ks[4], (DEC_BATCH, DEPTH, PAST_LEN, DA_HEADS, 2 * DA_HEAD_DIM), 1.0),
        'cache_da_v': nrm(ks[5], (DEC_BATCH, DEPTH, PAST_LEN, DA_HEADS, DA_V_DIM), 1.0),
        'c': nrm(ks[6], (DEC_BATCH, D_MODEL), 1.0),
        'c_ctx': nrm(ks[7], (D_MODEL,), 0.5),
        'w_ada': nrm(ks[8], (DEPTH, D_MODEL, 6 * D_MODEL), 0.5 * D_MODEL ** -0.5),
        'b_ada': nrm(ks[9], (DEPTH, 6 * D_MODEL), 0.01),
        'norm_mix': 1.0 + nrm(ks[10], (DEPTH, D_MODEL), 0.02),
        'norm_ffn': 1.0 + nrm(ks[11], (DEPTH, D_MODEL), 0.02),
        'w_in': nrm(ks[12], (DEPTH, D_MODEL, IN_W), D_MODEL ** -0.5),
        'hy_conv_w': nrm(ks[13], (DEPTH, 3, 3 * HY_WIDTH), 3 ** -0.5),
        'hy_conv_b': nrm(ks[14], (DEPTH, 3 * HY_WIDTH), 0.02),
        'hy_filt_w1': nrm(ks[15], (DEPTH, HY_POS_DIM, HY_FILT_HIDDEN), HY_POS_DIM ** -0.5),
        'hy_filt_b1': nrm(ks[16], (DEPTH, HY_FILT_HIDDEN), 0.02),
        'hy_filt_w2': nrm(ks[17], (DEPTH, HY_FILT_HIDDEN, HY_FILT_HIDDEN), HY_FILT_HIDDEN ** -0.5),
        'hy_filt_b2': nrm(ks[18], (DEPTH, HY_FILT_HIDDEN), 0.02),
        'hy_filt_w3': nrm(ks[19], (DEPTH, HY_FILT_HIDDEN, HY_ORDER * 2 * HY_WIDTH), HY_FILT_HIDDEN ** -0.5),
        'hy_filt_freq': 1.0 + nrm(ks[20], (DEPTH, HY_FILT_HIDDEN), 0.02),
        'hy_bias': nrm(ks[21], (DEPTH, HY_ORDER, HY_WIDTH), 0.5),
        'na_rpb': nrm(ks[22], (DEPTH, NA_HEADS, 2 * NA_WIN_ROWS - 1, 2 * NA_WIN_COLS - 1), 0.02),
        'da_lambda': nrm(ks[23], (DEPTH, 4, DA_HEAD_DIM), 0.1),
        'da_subln': 1.0 + nrm(ks[24], (DEPTH, DA_V_DIM), 0.02),
        'w_lift': nrm(ks[25], (DEPTH, N_BRANCH, BRANCH_W, D_MODEL), BRANCH_W ** -0.5),
        'w_out': nrm(ks[26], (DEPTH, D_MODEL, D_MODEL), D_MODEL ** -0.5),
        'w_ffn_in': nrm(ks[27], (DEPTH, D_MODEL, 2 * D_FF), D_MODEL ** -0.5),
        'w_ffn_out': nrm(ks[28], (DEPTH, D_FF, D_MODEL), D_FF ** -0.5),
        'norm_final': 1.0 + nrm(ks[29], (D_MODEL,), 0.02),
    }

def reference(x_prompt, x_sample, cache_na_k, cache_na_v, cache_da_k, cache_da_v, c, c_ctx,
              w_ada, b_ada, norm_mix, norm_ffn, w_in, hy_conv_w, hy_conv_b, hy_filt_w1, hy_filt_b1,
              hy_filt_w2, hy_filt_b2, hy_filt_w3, hy_filt_freq, hy_bias, na_rpb, da_lambda, da_subln,
              w_lift, w_out, w_ffn_in, w_ffn_out, norm_final):
    xp = x_prompt
    xs = x_sample
    na_ks, na_vs, da_ks, da_vs = [], [], [], []
    for l in range(DEPTH):
        lam_init = 0.8 - 0.6 * math.exp(-0.3 * l)
        mod_ctx = jax.nn.silu(c_ctx[None, :]) @ w_ada[l] + b_ada[l]
        mod_lat = jax.nn.silu(c) @ w_ada[l] + b_ada[l]
        lp = (norm_mix[l], norm_ffn[l], w_in[l], hy_conv_w[l], hy_conv_b[l], hy_filt_w1[l], hy_filt_b1[l],
              hy_filt_w2[l], hy_filt_b2[l], hy_filt_w3[l], hy_filt_freq[l], hy_bias[l], na_rpb[l],
              da_lambda[l], da_subln[l], w_lift[l], w_out[l], w_ffn_in[l], w_ffn_out[l])
        xp, ctx_kv = trunk_layer(xp, mod_ctx, None, lam_init, *lp)
        na_ks.append(ctx_kv[0])
        na_vs.append(ctx_kv[1])
        da_ks.append(ctx_kv[2])
        da_vs.append(ctx_kv[3])
        xs, _ = trunk_layer(xs, mod_lat, (cache_na_k[:, l], cache_na_v[:, l], cache_da_k[:, l], cache_da_v[:, l]),
                            lam_init, *lp)
    y_prompt = rmsnorm(xp, norm_final)
    y_sample = rmsnorm(xs, norm_final)
    new_na_k = jnp.stack(na_ks, axis=1)
    new_na_v = jnp.stack(na_vs, axis=1)
    new_da_k = jnp.stack(da_ks, axis=1)
    new_da_v = jnp.stack(da_vs, axis=1)
    return (y_prompt, y_sample, new_na_k, new_na_v, new_da_k, new_da_v)


_drawn_inputs = setup_inputs


def setup_inputs(seed=0):
    import zlib

    import numpy as np

    out = dict(_drawn_inputs(seed))
    spreads = {}
    factors = {'cache_na_k': 3.866,
     'cache_na_v': 3.27,
     'b_ada': 3.702,
     'norm_mix': 2.874,
     'norm_ffn': 7.301,
     'hy_conv_b': 8.0,
     'hy_filt_w1': 2.713,
     'hy_filt_b1': 8.0,
     'hy_filt_b2': 8.0,
     'hy_filt_w3': 2.747,
     'hy_filt_freq': 8.0,
     'na_rpb': 54.684,
     'da_lambda': 4.365,
     'da_subln': 8.0,
     'norm_final': 8.591,
     'cache_da_k': 8.0,
     'cache_da_v': 8.0}
    for name, (base, spread) in spreads.items():
        noise = np.random.default_rng([zlib.crc32(name.encode()), seed]).standard_normal(out[name].shape)
        drawn = base * np.exp(spread * noise) if base else spread * noise
        out[name] = jnp.asarray(drawn.astype(out[name].dtype))
    for name, factor in factors.items():
        out[name] = (out[name] * factor).astype(out[name].dtype)
    return out
```

```python
import math
from contextlib import ExitStack

import numpy as np
import concourse.bass as bass
from concourse import mybir

F32 = mybir.dt.float32
F32R = mybir.dt.float32r
BF16 = mybir.dt.bfloat16
ALU = mybir.AluOpType
ACT = mybir.ActivationFunctionType
AX = mybir.AxisListType.X

DEPTH = 2
D = 1024
KD = D // 128
C = 128
L = 512
T = C + L
HALF = T // 2
NT = T // 128
BW = 512
KB = BW // 128
HEADS = 8
GW = 64
ROWS = L // GW
BLK = 16
DFF = 2816
KF = DFF // 128
KFH = KF // 2
FEAT = 33
HID = 64
EPS = 1e-6
NEG = -1e30
DA_SCALE = 32 ** -0.5
TW = T + 2
LAT0 = C + 1

N_UHY, N_NA, N_DA, N_MERGE, N_OUT = 12, 12, 12, 36, 8
N_FIN, N_FOUT = 2 * KFH, KFH
S_UHY = 0
S_NA = S_UHY + N_UHY
S_DA = S_NA + N_NA
S_MERGE = S_DA + N_DA
S_OUT = S_MERGE + N_MERGE
S_FFN = S_OUT + N_OUT
STRIPS = S_FFN + 2 * (N_FIN + N_FOUT)
N_ADA = 6 * KD
ADA_SLOTS = 3

NA_BLOCKS = [[0, 1], [0, 1, 2], [1, 2, 3], [2, 3]]
NA_BIAS0 = [2, 1, 1, 0]
MASK0 = [0, 2, 5, 8]

P_BADA, P_NMIX, P_NFFN, P_CW, P_CB, P_HB, P_END = 0, 48, 56, 64, 100, 112, 120
R_SUB, R_LAM, R_LI, R_END = 0, 64, 192, 194
W_LA, W_LB, W_CA, W_CB, W_EPS, W_M0, W_END = 0, 1, 2, 3, 4, 5, 7


def build(nc, a):
    ctx = ExitStack()
    with ctx:
        def sem(name):
            return ctx.enter_context(nc.semaphore(name))

        top = [-(-nc.sbuf_base // 32) * 32]

        def keep(name, shape, dt):
            size = int(np.prod(shape[1:])) * (2 if dt == BF16 else 4)
            t = nc.alloc_sbuf_tensor_at(name, list(shape), dt, offset=top[0])
            top[0] += -(-size // 32) * 32
            return t

        x = keep("x", [128, KD, T], F32)
        wraw = [keep(f"wraw{i}", [128, KD, 128], F32) for i in range(2)]
        whi = [keep(f"whi{i}", [128, KD, 128], F32R) for i in range(2)]
        wlo = [keep(f"wlo{i}", [128, KD, 128], F32R) for i in range(2)]
        ident = keep("ident", [128, 128], F32)
        identb = keep("identb", [128, 128], BF16)
        ones = keep("ones", [128, 128], F32)
        maskb = keep("maskb", [128, 10, 128], BF16)
        ropec = keep("ropec", [128, L], F32)
        ropes = keep("ropes", [128, L], F32)
        wcol = keep("wcol", [128, W_END], F32)
        par = keep("par", [128, P_END], F32)
        rep = keep("rep", [128, R_END], F32)
        nfin = keep("nfin", [128, KD], F32)
        cin = keep("cin", [128, KD, 2], F32)
        csig = keep("csig", [128, KD, 2], F32)
        cs = keep("cs", [128, KD, 2], F32)
        mod = keep("mod", [128, 48, 2], F32)
        amod = keep("amod", [128, 2, KD, 2], F32)
        linv = keep("linv", [128, 16], F32)
        mx = keep("mx", [128, 4], F32)
        nmx = keep("nmx", [128, 4], F32)
        sums = keep("sums", [128, 2, 40], F32)
        rsum = keep("rsum", [128, 2, 40], F32)
        coef = keep("coef", [128, 4], F32)
        lamt = keep("lamt", [128, 72], F32)
        ssq = keep("ssq", [128, 40], F32)
        base = top[0]

        def at(name, kib, shape, dt=F32):
            size = int(np.prod(shape[1:])) * (2 if dt == BF16 else 4)
            off = base + int(round(kib * 1024))
            assert off % 4 == 0 and off + size <= nc.sbuf_usable_end, (name, off + size)
            return nc.alloc_sbuf_tensor_at(name, list(shape), dt, offset=off)

        hhi = at("hhi", 0, [128, KD, T], F32R)
        hlo = at("hlo", 20, [128, KD, T], F32R)
        xin = at("xin", 0, [128, NT, D])
        hfull = at("hfull", 0, [128, NT, 4, BW])
        habs = at("habs", 40, [128, 2, 4, BW])
        heo = at("heo", 56, [128, NT, 2, BW])
        ctab = at("ctab", 76, [128, 4, L])
        stab = at("stab", 84, [128, 4, L])
        sinv = at("sinv", 92, [128, 4, L])
        cctab = at("cctab", 100, [128, C])
        cstab = at("cstab", 100.5, [128, C])
        csinv = at("csinv", 101, [128, C])
        decay = at("decay", 101.5, [128, NT, BW])
        hst = [at(f"hst{i}", 111.5 + 6 * i, [128, 3, BW]) for i in range(2)]
        feats = at("feats", 123.5, [FEAT, T])
        habst = at("habst", 123.5, [128, BW])
        farg = at("farg", 126, [HID, T])
        fk = at("fk", 128.5, [HID, T])
        fw3 = at("fw3", 131, [HID, 4, BW])
        fw1 = at("fw1", 139, [FEAT, HID])
        fw2 = at("fw2", 139.25, [HID, HID])
        fvec = at("fvec", 139.5, [HID, 3])
        ada = [at(f"ada{i}", 140 + 4 * i, [128, KD, 128]) for i in range(ADA_SLOTS)]
        sq = [at(f"sq{i}", 40 + 2.5 * i, [128, T]) for i in range(2)]
        rstd = at("rstd", 45, [128, T])
        tn = [at(f"tn{i}", 47.5 + 2.5 * i, [128, T]) for i in range(2)]
        hf = [at(f"hf{i}", 52.5 + 2.5 * i, [128, T]) for i in range(2)]
        uhy = at("uhy", 40, [128, 12, TW])
        yhy_lo = at("yhy_lo", 40, [128, KB, T], F32R)
        zt = at("zt", 101.5, [128, NT, BW])
        yhy_hi = at("yhy_hi", 101.5, [128, KB, T], F32R)
        rawu = [at(f"rawu{i}", 111.5 + 2.625 * i, [128, TW + 2]) for i in range(2)]
        yr = [at(f"yr{i}", 116.75 + 4 * i, [128, 2, BW]) for i in range(2)]
        yt = at("yt", 124.75, [128, 4, BW])
        hld = [at(f"hld{i}", 132.75 + 6 * i, [128, 3, BW]) for i in range(2)]
        ztmp = [at(f"ztmp{i}", 144.75 + 2.625 * i, [128, TW]) for i in range(2)]
        naq = at("naq", 50.5, [128, KB, T])
        nak = at("nak", 60.5, [128, KB, T])
        yna_hi = at("yna_hi", 50.5, [128, KB, T], F32R)
        yna_lo = at("yna_lo", 60.5, [128, KB, T], F32R)
        nav = at("nav", 71, [128, NT, BW])
        nao = at("nao", 81, [128, NT, BW])
        nckt = at("nckt", 91, [128, BW])
        ncv = at("ncv", 93, [128, BW])
        nckT = at("nckT", 95, [128, KB, 128])
        bexp = at("bexp", 111.5, [128, HEADS, 5, 128])
        NRPB = 7 * 31 + 48
        rpbr = at("rpbr", 131.5, [128, HEADS, NRPB])
        nap = [at(f"nap{i}", 140 + 2 * i, [128, 512]) for i in range(2)]
        napt = [at(f"napt{i}", 144 + 2 * i, [128, 4, 128]) for i in range(2)]
        nkout = at("nkout", 148, [128, BW])
        daq = at("daq", 71, [128, KB, T])
        dak = at("dak", 81, [128, KB, T])
        yda_hi = at("yda_hi", 71, [128, KB, T], F32R)
        yda_lo = at("yda_lo", 81, [128, KB, T], F32R)
        dav = at("dav", 91, [128, NT, BW])
        dao = at("dao", 111.5, [128, NT, BW])
        dckt = at("dckt", 121.5, [128, BW])
        dcv = at("dcv", 123.5, [128, BW])
        dckz = at("dckz", 125.5, [128, 2, KB, 128])
        dkz = at("dkz", 129.5, [128, 2, KB, 128])
        dp1 = [at(f"dp1{i}", 133.5 + 5 * i, [128, 640]) for i in range(2)]
        dp2 = [at(f"dp2{i}", 136 + 5 * i, [128, 640]) for i in range(2)]
        dpt = [at(f"dpt{i}", 143.5 + 2.5 * i, [128, 5, 128]) for i in range(2)]
        dsw = at("dsw", 143.5, [128, L])
        draw = [at(f"draw{i}", 133.5 + 2.5 * i, [128, T]) for i in range(2)]
        dkout = at("dkout", 148.5, [128, BW])
        dosq = at("dosq", 125.5, [128, NT, BW])
        mghi = at("mghi", 111.5, [128, KD, T], F32R)
        mglo = at("mglo", 131.5, [128, KD, T], F32R)
        sig = [at(f"sig{i}", 91 + 2.5 * i, [128, T]) for i in range(2)]
        macc = [at(f"macc{i}", 96 + 2.5 * i, [128, T]) for i in range(2)]
        ahi = at("ahi", 57.5, [128, KFH, T], F32R)
        alo = at("alo", 86, [128, KFH, T], F32R)
        silu = [at(f"silu{i}", 114.5 + 2.5 * i, [128, T]) for i in range(2)]
        gact = [at(f"gact{i}", 119.5 + 2.5 * i, [128, T]) for i in range(2)]
        xo = at("xo", 57.5, [128, KD, T])
        yo = at("yo", 77.5, [128, NT, D])

        PS = ctx.enter_context(nc.psum_tensor("PS", [128, 8, 512], F32))
        PSF = PS[:, :, :].rearrange("p b n -> p (b n)")
        spectra = nc.dram_tensor("spectra", [2, NT, 128, 3, BW], F32, kind="Internal").ap()

        def pair(p):
            return PS[:, 2 * p:2 * p + 2, 0:HALF]

        def halves(ap):
            return ap.rearrange("p (h n) -> p h n", h=2)

        s_const = sem("consts_in")
        w_in = [sem(f"strip_in{i}") for i in range(2)]
        w_split = sem("strip_split")
        w_used = sem("strip_used")
        s_ada_turn = sem("ada_starts")
        s_turn = sem("split_starts")
        ada_in = [sem(f"ada_in{i}") for i in range(ADA_SLOTS)]
        ada_used = sem("ada_used")
        s_xT = sem("x_turned")
        s_xev = sem("x_kept")
        s_csig = sem("cond_sigmoid")
        s_cs = sem("cond_silu")
        s_merged_free = sem("merged_free")
        s_cleared = sem("layer_sems_cleared")
        s_out = sem("outputs_out")
        s_layer0 = s_layer_end = sem("layer_end")
        s_mod = sem("mod_sums")
        s_modr = sem("mod_ready")
        s_par = sem("params_in")
        s_fmm = sem("filter_mlp_sum")
        s_farg = sem("filter_arg")
        s_fsin = sem("filter_sin")
        s_hmm = sem("filter_sum")
        s_hev = sem("filter_kept")
        s_l1in = sem("filter_abs")
        s_l1 = sem("filter_l1")
        s_heo = sem("filter_even_odd")
        s_sp = sem("spectrum_sum")
        s_spev = sem("spectrum_kept")
        s_spout = [sem(f"spectrum_out{i}") for i in range(2)]
        s_sq = sem("squares")
        s_ss = sem("square_sums")
        s_rt = sem("root")
        s_rs = sem("rstd_ready")
        s_t = sem("normed")
        s_hi = sem("h_hi")
        s_h = sem("h_ready")
        s_u = sem("uhy_sum")
        s_uraw = sem("uhy_raw")
        s_uconv = sem("uhy_conv")
        s_ztm = sem("z_turned")
        s_zt = sem("zt_ready")
        s_z = sem("Z_sum")
        s_y = sem("Y_ready")
        s_hld = [sem(f"spectrum_in{i}") for i in range(2)]
        s_inv = sem("inverse_sum")
        s_zb = sem("z_bias")
        s_zn = sem("z_next")
        s_yhi = sem("yhy_hi_done")
        s_yhy = sem("yhy_done")
        s_nq = sem("na_qk_sum")
        s_nqe = sem("na_qk_kept")
        s_nv = sem("na_v_sum")
        s_nve = sem("na_v_kept")
        s_ncache = sem("na_cache_in")
        s_nct = sem("na_turned")
        s_nce = sem("na_turn_kept")
        s_bexp = sem("na_bias")
        s_ns = sem("na_scores")
        s_nm = sem("na_max")
        s_np = sem("na_probs")
        s_nt = sem("na_probs_turned")
        s_npt = sem("na_pt_ready")
        s_npv = sem("na_pv")
        s_no = sem("na_out_kept")
        s_noT = sem("na_out_turned")
        s_nyhi = sem("yna_hi_done")
        s_yna = sem("yna_done")
        s_dq = sem("da_qk_sum")
        s_dqe = sem("da_qk_raw")
        s_drope = sem("da_rope")
        s_dv = sem("da_v_sum")
        s_dve = sem("da_v_kept")
        s_dcache = sem("da_cache_in")
        s_dct = sem("da_turned")
        s_dce = sem("da_turn_kept")
        s_dkz = sem("da_own_keys")
        s_lamv = sem("lambda_dots")
        s_lame = sem("lambda_exp")
        s_ds = sem("da_scores")
        s_dm = sem("da_max")
        s_dp = sem("da_probs")
        s_da = sem("da_diff")
        s_dt = sem("da_diff_turned")
        s_dpt = sem("da_pt_ready")
        s_dpv = sem("da_pv")
        s_do = sem("da_out_kept")
        s_dss = sem("da_square_sums")
        s_dsr = sem("da_root")
        s_don = sem("da_out_normed")
        s_doT = sem("da_out_turned")
        s_dyhi = sem("yda_hi_done")
        s_yda = sem("yda_done")
        s_ko = sem("cache_k_out")
        s_lift = sem("lift_sum")
        s_lused = sem("lift_used")
        s_gate = sem("gate_sum")
        s_sig = sem("gate_sigmoid")
        s_macc = sem("merged")
        s_mhi = sem("merged_hi")
        s_mg = sem("merged_done")
        s_o = sem("out_sum")
        s_x = sem("x_added")
        s_fi = sem("ffn_in_sum")
        s_silu = sem("ffn_silu")
        s_gact = sem("ffn_product")
        s_ahi = sem("ffn_hi")
        s_act = sem("ffn_act")
        s_f = sem("ffn_out_sum")
        s_xf = sem("x_ffn_added")
        s_xo = sem("y_normed")
        s_yT = sem("y_turned")
        s_last = s_yo = sem("y_kept")

        layer_sems = range(s_layer0.num, s_last.num + 1)

        def end_layer(eng, lay, clears=False):
            eng.drain().then_inc(s_layer_end, 1)
            if clears:
                eng.wait_ge(s_layer_end, 3)
                eng.sem_clear(layer_sems)
                eng.sem_inc(s_cleared, 1)
            eng.wait_ge(s_cleared, lay + 1)

        block = ctx.enter_context(nc.Block())

        def grid(ap):
            return ap.rearrange("p (r b c) -> p b r c", r=ROWS, b=4)

        def rows_of(ap):
            return ap.rearrange("p (r c) -> p r c", c=BLK)

        def blocks_of(ap):
            return ap.rearrange("p (b r c) -> p b r c", b=4, c=BLK)

        @block.sync
        def _(sp):
            for dst, src in ((xin[:, :, :], a["x_in"]), (ident[:, :], a["ident"]), (cin[:, :, :], a["cond"]),
                             (identb[:, :], a["identb"]), (ones[:, :], a["ones"]), (maskb[:, :, :], a["maskb"]),
                             (ropec[:, :], a["ropec"]), (ropes[:, :], a["ropes"]), (wcol[:, :], a["wcol"]),
                             (nfin[:, :], a["nfin"])):
                sp.dma_start(dst, src).then_inc(s_const, 16)
            with sp.Fori(0, DEPTH) as lay:
                with sp.Fori(0, N_ADA // ADA_SLOTS) as i:
                    for j in range(ADA_SLOTS):
                        n = lay * N_ADA + i * ADA_SLOTS + j
                        sp.wait_ge(s_merged_free, lay + 1)
                        sp.sem_inc(s_ada_turn, 1)
                        sp.wait_ge(ada_used, n + 1)
                        sp.dma_start(ada[j][:, :, :].rearrange("p k n -> p (k n)"),
                                     a["w_ada"][n]).then_inc(ada_in[j], 16)
                with sp.Fori(0, STRIPS // 2) as i:
                    for j in range(2):
                        n = lay * STRIPS + i * 2 + j
                        sp.wait_ge(w_split, n + 1)
                        sp.dma_start(wraw[j][:, :, :].rearrange("p k n -> p (k n)"),
                                     a["w_strips"][n]).then_inc(w_in[j], 16)

        @block.gpsimd
        def _(pool):
            pool.sem_inc(w_split, 2)
            with pool.Fori(0, DEPTH * STRIPS // 2) as i:
                for j in range(2):
                    pool.wait_ge(w_in[j], 16 * (i + 1))
                    pool.wait_ge(w_used, 2 * i + j + 1)
                    pool.sem_inc(s_turn, 1)
                    raw, hi, lo = (w[j][:, :, :].rearrange("p k n -> p (k n)") for w in (wraw, whi, wlo))
                    nc.gpsimd.tensor_scalar(hi, raw, 1.0, None, ALU.mult)
                    pool.drain()
                    nc.gpsimd.tensor_tensor(lo, raw, hi, ALU.subtract).then_inc(w_split, 1)

        @block.tensor
        def _(pe):
            pe.sem_inc(w_used, 2)
            pe.sem_inc(ada_used, ADA_SLOTS)
            pe.sem_inc(s_merged_free, 1)

            def tiles_of(lay, idx, slot, work):
                pe.wait_ge(w_split, lay * STRIPS + idx + 3)
                for t, (kt, hi, lo, p, start, stop, done) in enumerate(work):
                    out = pair(p)
                    for m, (w, mv) in enumerate(((whi, hi), (whi, lo), (wlo, hi))):
                        for h in range(2):
                            ins = pe.matmul(out[:, h, :], w[slot][:, kt, :], mv[:, h * HALF:(h + 1) * HALF],
                                            start=start and m == 0, stop=stop and m == 2)
                    if done is not None:
                        ins.then_inc(done, 1)
                pe.drain().then_inc(w_used, 1) if done is not None else ins.then_inc(w_used, 1)

            def h_work(p, done, n=KD):
                return [(k, hhi[:, k, :], hlo[:, k, :], p, k == 0, k == KD - 1,
                         done if k == KD - 1 else None) for k in range(KD)]

            def v_strips(lay, idx0, done, free):
                pe.wait_ge(*free)
                for s in range(4):
                    slot = (idx0 + s) % 2
                    pe.wait_ge(w_split, lay * STRIPS + idx0 + s + 3)
                    for kk in range(2):
                        k = 2 * s + kk
                        wv = [w[slot][:, 4 * kk:4 * kk + 4, :] for w in (whi, wlo)]
                        for i in range(NT):
                            for m, (hp, w) in enumerate(((hhi, wv[0]), (hhi, wv[1]), (hlo, wv[0]))):
                                ins = pe.matmul(PS[:, i, :], hp[:, k, i * 128:(i + 1) * 128], w,
                                                start=(k == 0 and m == 0), stop=(k == KD - 1 and m == 2))
                    if s < 3:
                        ins.then_inc(w_used, 1)
                ins.then_inc(done, 1)
                pe.drain().then_inc(w_used, 1)

            def norm_sums(waits):
                for k in range(KD):
                    pe.wait_ge(s_sq, waits + k + 1)
                    for h in range(2):
                        ins = pe.matmul(PS[:, h, 0:HALF], ones[:, :], sq[k % 2][:, h * HALF:(h + 1) * HALF],
                                        start=(k == 0), stop=(k == KD - 1))
                    ins.then_inc(s_ss, 1)

            pe.wait_ge(s_const, 160)
            for n in range(2 * NT):
                i, g = n // 2, n % 2
                if n >= 8:
                    pe.wait_ge(s_xev, n - 7)
                for c in range(4):
                    ins = pe.transpose(PS[:, n % 8, c * 128:(c + 1) * 128],
                                       xin[:, i, (4 * g + c) * 128:(4 * g + c + 1) * 128], ident[:, :])
                ins.then_inc(s_xT, 1)
            pe.wait_ge(s_xev, 2 * NT)
            pe.wait_ge(s_cs, 1)

            with pe.Fori(0, DEPTH) as lay:
                for s, n in ((s_uraw, 4), (s_nqe, 4), (s_dqe, 4), (s_lused, 2), (s_sig, 2), (s_gact, 2)):
                    pe.sem_inc(s, n)
                ada_n = [0]

                def ada_strips(n):
                    for _ in range(n):
                        m = ada_n[0]
                        if m == N_ADA:
                            return
                        ada_n[0] += 1
                        j = m % ADA_SLOTS
                        pe.wait_ge(ada_in[j], 16 * (lay * (N_ADA // ADA_SLOTS) + m // ADA_SLOTS + 1))
                        for k in range(KD):
                            ins = pe.matmul(PS[:, 7, 2 * m:2 * m + 2], ada[j][:, k, :], cs[:, k, :],
                                            start=(k == 0), stop=(k == KD - 1))
                        ins.then_inc(ada_used, 1)

                pe.wait_ge(s_par, 16 * 14)
                for h in range(2):
                    ins = pe.matmul(PS[0:HID, h, 0:HALF], fw1[:, :], feats[:, h * HALF:(h + 1) * HALF],
                                    start=True, stop=True)
                ins.then_inc(s_fmm, 1)
                ada_strips(3)
                pe.wait_ge(s_fsin, 1)
                for h in range(2):
                    ins = pe.matmul(PS[0:HID, h, 0:HALF], fw2[:, :], farg[:, h * HALF:(h + 1) * HALF],
                                    start=True, stop=True)
                ins.then_inc(s_fmm, 1)
                ada_strips(3)
                pe.wait_ge(s_fsin, 2)
                for n in range(4 * NT):
                    i, q = n // 4, n % 4
                    if n >= 4:
                        pe.wait_ge(s_hev, n - 3)
                    pe.matmul(PS[:, n % 4, :], farg[:, i * 128:(i + 1) * 128], fw3[:, q, :],
                              start=True, stop=True).then_inc(s_hmm, 1)
                    if n % 2:
                        ada_strips(1)
                ada_strips(6)
                pe.wait_ge(s_l1in, 1)
                for o in range(2):
                    for q in range(2):
                        for c in range(KB):
                            col = 8 * o + 4 * q + c
                            for d in range(2):
                                ins = pe.matmul(PS[:, 6, col:col + 1], habs[:, q, 2 * o + d, c * 128:(c + 1) * 128],
                                                ones[:, 0:1], start=(d == 0), stop=(d == 1))
                ins.then_inc(s_l1, 1)
                for o in range(2):
                    pe.wait_ge(s_heo, o + 1)
                    for n, (kind, fc) in enumerate(SPECTRA):
                        g = 12 * o + n
                        if g >= 4:
                            pe.wait_ge(s_spev, g - 3)
                        out = PS[:, g % 4, :] if kind != "alt" else PS[0:1, g % 4, :]
                        eo = 1 if kind == "B" else 0
                        tiles = [0] if fc == 0 else [1, 2, 3, 4]
                        for r, i in enumerate(tiles):
                            if fc == 0:
                                w = {"A": cctab[:, :], "B": cstab[:, :], "alt": cstab[:, 0:1]}[kind]
                            else:
                                cols = slice((fc - 1) * 128, fc * 128) if kind != "alt" else slice(0, 1)
                                w = (ctab if kind == "A" else stab)[:, r, cols]
                            ins = pe.matmul(out, w, heo[:, i, eo, :], start=(r == 0), stop=(r == len(tiles) - 1))
                        ins.then_inc(s_sp, 1)
                        ada_strips(2)
                ada_strips(N_ADA)
                pe.drain().then_inc(s_mod, 1)

                pe.wait_ge(s_spev, 24)
                norm_sums(0)
                pe.wait_ge(s_rt, 1)

                with pe.Fori(0, N_UHY // 4) as i:
                    for j in range(4):
                        n = i * 4 + j
                        if j == 0:
                            pe.wait_ge(s_h, KD)
                        pe.wait_ge(s_uraw, n + 1)
                        tiles_of(lay, S_UHY + n, j % 2, h_work(j, s_u))

                for o in range(2):
                    for i in range(NT):
                        if o == 0:
                            pe.wait_ge(s_uconv, 4)
                            if i == 0:
                                pe.wait_ge(s_uraw, 12 + 4)
                        else:
                            pe.wait_ge(s_zn, 4)
                        if i == 4:
                            pe.wait_ge(s_zt, 5 * o + 1)
                        col = 0 if i == 0 else LAT0 + (i - 1) * 128
                        for c in range(KB):
                            ins = pe.transpose(PS[:, i % 4, c * 128:(c + 1) * 128], uhy[:, c, col:col + 128],
                                               ident[:, :])
                        ins.then_inc(s_ztm, 1)
                    pe.wait_ge(s_zt, 5 * o + 5)

                    def forward(s, fc):
                        if s >= 2:
                            pe.wait_ge(s_y, 5 * o + s - 1)
                        for part, (lt, ct) in enumerate(((ctab, cctab), (stab, cstab))):
                            out = PS[:, 2 * (s % 2) + part, :]
                            if fc == 0:
                                ins = pe.matmul(out, ct[:, :], zt[:, 0, :], start=True, stop=True)
                            else:
                                for r in range(4):
                                    ins = pe.matmul(out, lt[:, r, (fc - 1) * 128:fc * 128], zt[:, 1 + r, :],
                                                    start=(r == 0), stop=(r == 3))
                        ins.then_inc(s_z, 1)

                    def inverse(s, fc):
                        pe.wait_ge(s_y, 5 * o + s + 1)
                        for c in range(KB):
                            for part, (lt, ct) in enumerate(((ctab, cctab), (sinv, csinv))):
                                w = yr[s % 2][:, part, c * 128:(c + 1) * 128]
                                if fc == 0:
                                    ins = pe.matmul(PS[:, 2, c * 128:(c + 1) * 128], w, ct[:, :],
                                                    start=(part == 0), stop=(part == 1))
                                else:
                                    ins = pe.matmul(PS[:, 4 + c, :], w, lt[:, fc - 1, :],
                                                    start=(fc == 1 and part == 0), stop=(fc == 4 and part == 1))
                            if fc == 4:
                                ins.then_inc(s_inv, 1)
                        if fc == 0:
                            ins.then_inc(s_inv, 1)

                    for s, fc in enumerate(FC_ORDER):
                        forward(s, fc)
                        if s >= 1:
                            inverse(s - 1, FC_ORDER[s - 1])
                    inverse(NT - 1, FC_ORDER[NT - 1])

                pe.wait_ge(s_yhy, 4)
                with pe.Fori(0, 2) as i:
                    for j in range(4):
                        pe.wait_ge(s_nqe, i * 4 + j + 1)
                        tiles_of(lay, S_NA + i * 4 + j, j % 2, h_work(j, s_nq))

                v_strips(lay, S_NA + 8, s_nv, (s_nqe, 12))
                pe.wait_ge(s_ncache, 48)
                for c in range(KB):
                    ins = pe.transpose(PS[:, 6, c * 128:(c + 1) * 128], nckt[:, c * 128:(c + 1) * 128], ident[:, :])
                ins.then_inc(s_nct, 1)
                for c in range(KB):
                    ins = pe.transpose(PS[:, 7, c * 128:(c + 1) * 128], nak[:, c, 0:C], ident[:, :])
                ins.then_inc(s_nct, 1)
                pe.wait_ge(s_nve, 5)
                pe.wait_ge(s_nce, 2)

                def na_scores(n):
                    qb, h = n // HEADS, n % HEADS
                    if n >= 2:
                        pe.wait_ge(s_np, n - 1)
                    r0, ch = 64 * (h % 2), h // 2
                    out = PS[:, n % 2, :]
                    q = naq[r0:r0 + 64, ch, qb * 128:(qb + 1) * 128]
                    if qb == 0:
                        pe.matmul(out[:, 0:128], q, nak[r0:r0 + 64, ch, 0:C],
                                  start=True, stop=True).then_inc(s_ns, 1)
                        return
                    j = qb - 1
                    b0, nb = NA_BLOCKS[j][0], len(NA_BLOCKS[j])
                    lat0, cache0 = (128, 0) if j == 3 else (0, nb * 128)
                    lat = out[:, lat0:lat0 + nb * 128]
                    pe.matmul(lat, q, nak[r0:r0 + 64, ch, C + b0 * 128:C + (b0 + nb) * 128],
                              start=True, stop=False)
                    pe.matmul(lat, identb[:, :], maskb[:, MASK0[j]:MASK0[j] + nb, :], start=False, stop=True)
                    pe.matmul(out[:, cache0:cache0 + 128], q, nckT[r0:r0 + 64, ch, :],
                              start=True, stop=True).then_inc(s_ns, 1)

                def na_turn(n):
                    qb = n // HEADS
                    nk = 1 if qb == 0 else len(NA_BLOCKS[qb - 1]) + 1
                    pe.wait_ge(s_np, n + 1)
                    if n >= 2:
                        pe.wait_ge(s_npt, n - 1)
                    for i in range(nk):
                        ins = pe.transpose(PS[:, 2 + n % 2, i * 128:(i + 1) * 128],
                                           nap[n % 2][:, i * 128:(i + 1) * 128], ident[:, :])
                    ins.then_inc(s_nt, 1)

                def na_pv(n):
                    qb, h = n // HEADS, n % HEADS
                    pe.wait_ge(s_npt, n + 1)
                    if h == 0 and qb >= 2:
                        pe.wait_ge(s_no, qb - 1)
                    hc = slice(h * 64, (h + 1) * 64)
                    if qb == 0:
                        vs = [nav[:, 0, hc]]
                    else:
                        vs = [nav[:, 1 + b, hc] for b in NA_BLOCKS[qb - 1]]
                        vs = [ncv[:, hc]] + vs if qb == 4 else vs + [ncv[:, hc]]
                    for i, v in enumerate(vs):
                        ins = pe.matmul(PS[:, 4 + qb % 2, hc], napt[n % 2][:, i, :], v,
                                        start=(i == 0), stop=(i == len(vs) - 1))
                    ins.then_inc(s_npv, 1)

                na_scores(0)
                for n in range(40):
                    if n + 1 < 40:
                        na_scores(n + 1)
                    na_turn(n)
                    if n >= 1:
                        na_pv(n - 1)
                na_pv(39)
                for qb in range(NT):
                    pe.wait_ge(s_no, qb + 1)
                    if qb >= 2:
                        pe.wait_ge(s_yna, qb - 1)
                    for c in range(KB):
                        ins = pe.transpose(PS[:, 6 + qb % 2, c * 128:(c + 1) * 128],
                                           nao[:, qb, c * 128:(c + 1) * 128], ident[:, :])
                    ins.then_inc(s_noT, 1)

                pe.wait_ge(s_yna, 5)
                with pe.Fori(0, 2) as i:
                    for j in range(4):
                        pe.wait_ge(s_dqe, i * 4 + j + 1)
                        tiles_of(lay, S_DA + i * 4 + j, j % 2, h_work(j, s_dq))
                v_strips(lay, S_DA + 8, s_dv, (s_dqe, 12))
                pe.wait_ge(s_dcache, 32)
                for c in range(KB):
                    ins = pe.transpose(PS[:, 6, c * 128:(c + 1) * 128], dckt[:, c * 128:(c + 1) * 128], ident[:, :])
                ins.then_inc(s_dct, 1)
                pe.wait_ge(s_drope, 8)
                for c in range(KB):
                    ins = pe.transpose(PS[:, 7, c * 128:(c + 1) * 128], dak[:, c, 0:C], ident[:, :])
                ins.then_inc(s_dct, 1)
                pe.wait_ge(s_dve, 5)
                pe.wait_ge(s_dce, 2)
                pe.wait_ge(s_dkz, 1)

                def da_scores(n):
                    qb, h = n // HEADS, n % HEADS
                    if n >= 2:
                        pe.wait_ge(s_dp, n - 1)
                        pe.wait_ge(s_dpt, n - 1)
                    b = 3 * (n % 2)
                    for m in range(2):
                        f0 = h * 64 + m * 32
                        r0, ch = f0 % 128, f0 // 128
                        q = daq[r0:r0 + 32, ch, qb * 128:(qb + 1) * 128]
                        r1 = r0 - 32 * m
                        own = (dkz if qb == 0 else dckz)[r1:r1 + 64, m, ch, :]
                        if qb:
                            pe.matmul(PS[:, b + 2 * m, :], q, dak[r0:r0 + 32, ch, C:T], start=True, stop=True)
                        ins = pe.matmul(PS[:, b + 1, 384 * m:384 * m + 128],
                                        daq[r1:r1 + 64, ch, qb * 128:(qb + 1) * 128], own, start=True, stop=True)
                    ins.then_inc(s_ds, 1)

                def da_turn(n):
                    qb = n // HEADS
                    pe.wait_ge(s_da, n + 1)
                    if n >= 1:
                        pe.wait_ge(s_dpt, n)
                    if qb:
                        for i in range(4):
                            pe.transpose(PS[:, 6, i * 128:(i + 1) * 128], dp1[n % 2][:, i * 128:(i + 1) * 128],
                                         ident[:, :])
                    pe.transpose(PS[:, 3 * (n % 2) + 1, 128:256], dp1[n % 2][:, 512:640],
                                 ident[:, :]).then_inc(s_dt, 1)

                def da_pv(n):
                    qb, h = n // HEADS, n % HEADS
                    pe.wait_ge(s_dpt, n + 1)
                    if h == 0 and qb >= 1:
                        pe.wait_ge(s_do, qb)
                    hc = slice(h * 64, (h + 1) * 64)
                    vs = [(4, dav[:, 0, hc])] if qb == 0 else \
                        [(i, dav[:, 1 + i, hc]) for i in range(4)] + [(4, dcv[:, hc])]
                    for r, (i, v) in enumerate(vs):
                        ins = pe.matmul(PS[:, 7, hc], dpt[n % 2][:, i, :], v, start=(r == 0), stop=(r == len(vs) - 1))
                    ins.then_inc(s_dpv, 1)

                da_scores(0)
                for n in range(40):
                    if n + 1 < 40:
                        da_scores(n + 1)
                    da_turn(n)
                    if n >= 1:
                        da_pv(n - 1)
                da_pv(39)
                pe.wait_ge(s_don, 1)
                for qb in range(NT):
                    if qb >= 2:
                        pe.wait_ge(s_yda, qb - 1)
                    for c in range(KB):
                        ins = pe.transpose(PS[:, qb % 2, c * 128:(c + 1) * 128],
                                           dao[:, qb, c * 128:(c + 1) * 128], ident[:, :])
                    ins.then_inc(s_doT, 1)
                pe.wait_ge(s_yda, 5)

                ys = ((yhy_hi, yhy_lo), (yna_hi, yna_lo), (yda_hi, yda_lo))
                with pe.Fori(0, 2) as i:
                    for mp in range(2):
                        for b in range(3):
                            g = i * 12 + mp * 6 + b * 2
                            s0 = S_MERGE + i * 18 + mp * 9 + b * 3
                            sl = (mp * 9 + b * 3) % 2
                            pe.wait_ge(s_lused, g + 2)
                            tiles_of(lay, s0, sl, [
                                (4 * m + k, ys[b][0][:, k, :], ys[b][1][:, k, :], m, k == 0, k == KB - 1,
                                 s_lift if k == KB - 1 else None) for m in range(2) for k in range(KB)])
                            for m in range(2):
                                pe.wait_ge(s_sig, g + m + 1)
                                tiles_of(lay, s0 + 1 + m, (sl + 1 + m) % 2, h_work(2 + m, s_gate))

                pe.wait_ge(s_mg, 8)
                pe.wait_ge(s_sig, 26)
                for m in range(KD):
                    if m >= 4:
                        pe.wait_ge(s_x, m - 3)
                    tiles_of(lay, S_OUT + m, m % 2, [
                        (k, mghi[:, k, :], mglo[:, k, :], m % 4, k == 0, k == KD - 1,
                         s_o if k == KD - 1 else None) for k in range(KD)])

                pe.wait_ge(s_x, 8)
                norm_sums(8)
                pe.wait_ge(s_rt, 2)
                pe.wait_ge(s_h, 16)

                for f in range(2):
                    s0 = S_FFN + f * (N_FIN + N_FOUT)
                    if f:
                        pe.wait_ge(s_xf, 8)

                    def ffn_in(i, j, slot):
                        pe.wait_ge(s_gact, f * KFH + i * 2 + j + 1)
                        for u in range(2):
                            tiles_of(lay, s0 + (i * 2 + j) * 2 + u, (slot + u) % 2,
                                     h_work(2 * j + u, s_fi if u else None))

                    with pe.Fori(0, KFH // 2) as i:
                        for j in range(2):
                            ffn_in(i, j, s0 % 2)
                    ffn_in(KFH // 2, 0, s0 % 2)
                    pe.wait_ge(s_act, (f + 1) * KFH)
                    s1 = s0 + N_FIN
                    for st in range(N_FOUT):
                        work = []
                        for kt in range(KD):
                            m, k = divmod(st * KD + kt, KFH)
                            work.append((kt, ahi[:, k, :], alo[:, k, :], m % 4, k == 0, k == KFH - 1,
                                         s_f if k == KFH - 1 else None))
                        for m in range(4, KD):
                            if (m * KFH) // KD == st:
                                pe.wait_ge(s_xf, f * 8 + m - 3)
                        tiles_of(lay, s1 + st, (s1 + st) % 2, work)
                end_layer(pe, lay)

            norm_sums(0)
            for n in range(2 * NT):
                i, g = n // 2, n % 2
                pe.wait_ge(s_xo, 8 if g else 4)
                if n >= 6:
                    pe.wait_ge(s_yo, n - 5)
                for c in range(4):
                    ins = pe.transpose(PS[:, 2 + n % 6, c * 128:(c + 1) * 128],
                                       xo[:, 4 * g + c, i * 128:(i + 1) * 128], ident[:, :])
                ins.then_inc(s_yT, 1)

        @block.scalar
        def _(act):
            A = nc.scalar.activation

            def norm_squares(waits, xwait):
                for k in range(KD):
                    if xwait is not None:
                        act.wait_ge(xwait[0], xwait[1] + k + 1)
                    if k >= 2:
                        act.wait_ge(s_ss, waits + k - 1)
                    A(sq[k % 2][:, :], x[:, k, :], ACT.Square).then_inc(s_sq, 1)

            def norm_root(waits):
                act.wait_ge(s_ss, waits + KD)
                A(halves(rstd[:, :]), PS[:, 0:2, 0:HALF], ACT.Sqrt, bias=wcol[:, W_EPS:W_EPS + 1],
                  scale=1.0 / D).then_inc(s_rt, 1)

            def norm_apply(waits, which):
                shift = 24 * which
                for k in range(KD):
                    act.wait_ge(s_t, waits + k + 1)
                    if k >= 2:
                        act.wait_ge(s_h, waits + k - 1)
                    for sgm, cols in enumerate((slice(0, C), slice(C, T))):
                        A(hf[k % 2][:, cols], tn[k % 2][:, cols], ACT.Identity,
                          bias=mod[:, shift + k, sgm:sgm + 1], scale=amod[:, which, k, sgm:sgm + 1])
                    act.drain()
                    A(hhi[:, k, :], hf[k % 2][:, :], ACT.Copy).then_inc(s_hi, 1)

            act.wait_ge(s_const, 160)
            A(csig[:, :, :], cin[:, :, :], ACT.Sigmoid).then_inc(s_csig, 1)
            act.wait_ge(s_xev, 2 * NT)
            with act.Fori(0, DEPTH) as lay:
                for dst, src in ((par[:, :], a["par"][lay]), (rep[:, :], a["rep"][lay]),
                                 (fw1[:, :], a["fw1"][lay]), (fw2[:, :], a["fw2"][lay]),
                                 (fw3[:, :, :], a["fw3"][lay]), (fvec[:, :], a["fvec"][lay]),
                                 (feats[:, :], a["feats"]), (decay[:, :, :], a["decay"]),
                                 (ctab[:, :, :], a["ctab"]), (stab[:, :, :], a["stab"]),
                                 (sinv[:, :, :], a["sinv"]), (cctab[:, :], a["cctab"]),
                                 (cstab[:, :], a["cstab"]), (csinv[:, :], a["csinv"])):
                    act.dma_start(dst, src).then_inc(s_par, 16)
                for n in range(2):
                    act.wait_ge(s_farg, n + 1)
                    A(farg[:, :], farg[:, :], ACT.Sin).then_inc(s_fsin, 1)
                for o in range(2):
                    for n, (kind, fc) in enumerate(SPECTRA):
                        g = 12 * o + n
                        act.wait_ge(s_sp, g + 1)
                        buf = 5 * o + fc
                        st = hst[buf % 2]
                        ps = PS[:, g % 4, :]
                        seq = L if fc else C
                        if kind == "A":
                            if buf >= 2:
                                act.wait_ge(s_spout[buf % 2], 16 * (buf // 2))
                            w = wcol[:, (W_LA if fc else W_CA):(W_LA if fc else W_CA) + 1] if fc < 2 else 1.0 / L
                            ins = A(st[:, 0, :], ps, ACT.Copy, scale=w)
                            if fc < 2:
                                ins = A(st[:, 2, :], ps, ACT.Copy, scale=w)
                        elif kind == "B":
                            w = wcol[:, (W_LB if fc else W_CB):(W_LB if fc else W_CB) + 1] if fc < 2 else 1.0 / L
                            ins = A(st[:, 1, :], ps, ACT.Copy, scale=w)
                        else:
                            act.drain()
                            ins = A(st[0:1, 2, :], ps[0:1, :], ACT.Copy, scale=0.5 / seq)
                        ins.then_inc(s_spev, 1)
                        if kind == "alt" or (kind == "B" and fc >= 2):
                            parts = 3 if fc < 2 else 2
                            act.wait_ge(s_spev, g + 1)
                            act.dma_start(spectra[o, fc, :, 0:parts, :], st[:, 0:parts, :]).then_inc(
                                s_spout[buf % 2], 16)
                act.wait_ge(s_l1, 1)
                norm_squares(0, None)
                norm_root(0)
                act.wait_ge(s_modr, 1)
                norm_apply(0, 0)
                for b in range(2):
                    act.wait_ge(s_spout[b], 16 * 5)
                for b in range(2):
                    for col in (0, LAT0, LAT0 + 1 + L):
                        nc.scalar.activation(rawu[b][:, col:col + 1], ones[:, 0:1], ACT.Copy, scale=0.0)
                act.wait_ge(s_h, 8)
                for n in range(12):
                    act.wait_ge(s_u, n + 1)
                    if n >= 2:
                        act.wait_ge(s_uconv, n - 1)
                    r = rawu[n % 2]
                    g = grid(r[:, LAT0 + 1:LAT0 + 1 + L])
                    p0, p1 = PS[:, 2 * (n % 4), :], PS[:, 2 * (n % 4) + 1, :]
                    A(r[:, 1:1 + C], p0[:, 0:C], ACT.Copy)
                    A(g[:, 0], rows_of(p0[:, C:C + 128]), ACT.Copy)
                    A(g[:, 1, 0:4], rows_of(p0[:, C + 128:HALF]), ACT.Copy)
                    A(g[:, 1, 4:8], rows_of(p1[:, 0:64]), ACT.Copy)
                    A(g[:, 2:4], p1[:, 64:HALF].rearrange("p (b r c) -> p b r c", b=2, c=BLK),
                      ACT.Copy).then_inc(s_uraw, 1)
                for o in range(2):
                    def load_spectrum(s):
                        fc = FC_ORDER[s]
                        parts = 3 if fc < 2 else 2
                        u = 5 * o + s
                        if u >= 2:
                            act.wait_ge(s_y, u - 1)
                        act.dma_start(hld[u % 2][:, 0:parts, :], spectra[o, fc, :, 0:parts, :]).then_inc(
                            s_hld[u % 2], 16)

                    load_spectrum(0)
                    load_spectrum(1)
                    for i in range(NT):
                        act.wait_ge(s_ztm, 5 * o + i + 1)
                        A(zt[:, i, :], PS[:, i % 4, :], ACT.Copy).then_inc(s_zt, 1)
                    for s in range(2, NT):
                        load_spectrum(s)
                    for c in range(KB):
                        if c >= 2:
                            act.wait_ge(s_zn, 4 * o + c - 1)
                        if o == 0 and c == 0:
                            act.wait_ge(s_uconv, 12)
                        A(ztmp[c % 2][:, 0:T + 1], uhy[:, c, 0:T + 1], ACT.Copy,
                          scale=par[:, P_HB + 4 * o + c:P_HB + 4 * o + c + 1]).then_inc(s_zb, 1)
                        if o == 1:
                            act.wait_ge(s_zn, 4 * o + c + 1)
                            if c == 0:
                                act.wait_ge(s_z, 10)
                            A(yhy_hi[:, c, 0:C], ztmp[c % 2][:, 0:C], ACT.Copy)
                            A(blocks_of(yhy_hi[:, c, C:T]), grid(ztmp[c % 2][:, LAT0:LAT0 + L]), ACT.Copy).then_inc(s_yhi, 1)
                act.wait_ge(s_yhy, 4)
                act.dma_start(nckt[:, :], a["cache_na_k"][lay]).then_inc(s_ncache, 16)
                act.dma_start(ncv[:, :], a["cache_na_v"][lay]).then_inc(s_ncache, 16)
                act.dma_start(rpbr[:, :, :], a["rpb"][lay]).then_inc(s_ncache, 16)
                for n in range(8):
                    act.wait_ge(s_nq, n + 1)
                    dst, sc = (naq, 0.125) if n < 4 else (nak, 1.0)
                    A(halves(dst[:, n % 4, :]), pair(n % 4), ACT.Copy, scale=sc).then_inc(s_nqe, 1)
                act.wait_ge(s_nv, 1)
                for i in range(NT):
                    A(nav[:, i, :], PS[:, i, :], ACT.Copy).then_inc(s_nve, 1)
                act.wait_ge(s_nve, 1)
                act.dma_start(a["new_na_v"][lay], nav[:, 0, :]).then_inc(s_ko, 16)
                act.wait_ge(s_nct, 1)
                A(nckT[:, :, :].rearrange("p c n -> p (c n)"), PS[:, 6, :], ACT.Copy).then_inc(s_nce, 1)
                act.wait_ge(s_nct, 2)
                A(nkout[:, :], PS[:, 7, :], ACT.Copy).then_inc(s_nce, 1)
                act.wait_ge(s_nce, 2)
                act.dma_start(a["new_na_k"][lay], nkout[:, :]).then_inc(s_ko, 16)
                for n in range(40):
                    qb = n // HEADS
                    nk = 128 * (1 if qb == 0 else len(NA_BLOCKS[qb - 1]) + 1)
                    act.wait_ge(s_nm, n + 1)
                    if qb == 0 and n >= 2:
                        act.wait_ge(s_nt, n - 1)
                    src = PS[:, n % 2, 0:nk] if qb == 0 else nap[n % 2][:, 0:nk]
                    A(nap[n % 2][:, 0:nk], src, ACT.Exp, bias=nmx[:, n % 2:n % 2 + 1], scale=1.0,
                      accum_out=sums[:, 0, n:n + 1]).then_inc(s_np, 1)
                for qb in range(NT):
                    act.wait_ge(s_noT, qb + 1)
                    src = PS[:, 6 + qb % 2, :]
                    A(yna_hi[:, :, qb * 128:(qb + 1) * 128], src.rearrange("p (c n) -> p c n", c=KB),
                      ACT.Copy).then_inc(s_nyhi, 1)
                act.wait_ge(s_yna, 5)
                act.wait_ge(s_ko, 16 * 2)
                act.dma_start(dckt[:, :], a["cache_da_k"][lay]).then_inc(s_dcache, 16)
                act.dma_start(dcv[:, :], a["cache_da_v"][lay]).then_inc(s_dcache, 16)
                act.wait_ge(s_lamv, 1)
                A(lamt[:, 66:68], lamt[:, 64:66], ACT.Exp).then_inc(s_lame, 1)
                for n in range(8):
                    act.wait_ge(s_dq, n + 1)
                    if n >= 2:
                        act.wait_ge(s_drope, n - 1)
                    A(halves(draw[n % 2][:, :]), pair(n % 4), ACT.Copy).then_inc(s_dqe, 1)
                act.wait_ge(s_dv, 1)
                for i in range(NT):
                    A(dav[:, i, :], PS[:, i, :], ACT.Copy).then_inc(s_dve, 1)
                act.wait_ge(s_dve, 1)
                act.dma_start(a["new_da_v"][lay], dav[:, 0, :]).then_inc(s_ko, 16)
                act.wait_ge(s_dct, 1)
                for m in range(2):
                    ins = A(dckz[:, m].rearrange("p c n -> p (c n)"), PS[:, 6, :], ACT.Copy,
                            scale=wcol[:, W_M0 + m:W_M0 + m + 1])
                ins.then_inc(s_dce, 1)
                act.wait_ge(s_dct, 2)
                A(dkout[:, :], PS[:, 7, :], ACT.Copy).then_inc(s_dce, 1)
                act.wait_ge(s_dce, 2)
                act.dma_start(a["new_da_k"][lay], dkout[:, :]).then_inc(s_ko, 16)

                def da_exp(n):
                    qb, b = n // HEADS, 3 * (n % 2)
                    act.wait_ge(s_dm, n + 1)
                    if n >= 2:
                        act.wait_ge(s_dt, n - 1)
                    lo1, hi2 = (0, 640) if qb else (512, 128)
                    s1 = PSF[:, 512 * b + lo1:512 * b + 640]
                    s2 = PSF[:, 512 * (b + 1) + 384:512 * (b + 1) + 384 + hi2]
                    q = 2 * (n % 2)
                    A(dp1[n % 2][:, lo1:640], s1, ACT.Exp, bias=nmx[:, q:q + 1], scale=DA_SCALE,
                      accum_out=sums[:, 0, n:n + 1])
                    A(dp2[n % 2][:, 0:hi2], s2, ACT.Exp, bias=nmx[:, q + 1:q + 2], scale=DA_SCALE,
                      accum_out=sums[:, 1, n:n + 1]).then_inc(s_dp, 1)

                def da_keep(n):
                    qb = n // HEADS
                    act.wait_ge(s_dt, n + 1)
                    if n >= 2:
                        act.wait_ge(s_dpv, n - 1)
                    if qb:
                        A(dpt[n % 2][:, 0:4, :].rearrange("p i n -> p (i n)"), PS[:, 6, :], ACT.Copy)
                    A(dpt[n % 2][:, 4, :], PS[:, 3 * (n % 2) + 1, 128:256], ACT.Copy).then_inc(s_dpt, 1)

                for n in range(40):
                    da_exp(n)
                    if n >= 1:
                        da_keep(n - 1)
                da_keep(39)
                act.wait_ge(s_dss, 1)
                A(ssq[:, :], ssq[:, :], ACT.Sqrt, bias=wcol[:, W_EPS:W_EPS + 1],
                  scale=1.0 / 64).then_inc(s_dsr, 1)
                for qb in range(NT):
                    act.wait_ge(s_doT, qb + 1)
                    A(yda_hi[:, :, qb * 128:(qb + 1) * 128], PS[:, qb % 2, :].rearrange("p (c n) -> p c n", c=KB),
                      ACT.Copy).then_inc(s_dyhi, 1)
                act.wait_ge(s_ko, 16 * 4)
                with act.Fori(0, 4) as i:
                    for b in range(3):
                        for m in range(2):
                            g = i * 6 + b * 2 + m
                            act.wait_ge(s_gate, g + 1)
                            act.wait_ge(s_lused, g + 1)
                            A(halves(sig[m][:, :]), pair(2 + m), ACT.Sigmoid).then_inc(s_sig, 1)
                    for m in range(2):
                        act.wait_ge(s_macc, i * 2 + m + 1)
                        A(mghi[:, 2 * i + m, :], macc[m][:, :], ACT.Copy).then_inc(s_mhi, 1)
                norm_squares(8, (s_x, 0))
                norm_root(8)
                norm_apply(8, 1)
                for f in range(2):
                    if f:
                        act.wait_ge(s_xf, 8)

                    def ffn_act(i, j):
                        c = f * KFH + i * 2 + j
                        act.wait_ge(s_fi, c + 1)
                        act.wait_ge(s_gact, c + 1)
                        A(halves(silu[j][:, :]), pair(2 * j), ACT.Silu).then_inc(s_silu, 1)
                        act.wait_ge(s_gact, c + 3)
                        A(ahi[:, i * 2 + j, :], gact[j][:, :], ACT.Copy).then_inc(s_ahi, 1)

                    with act.Fori(0, KFH // 2) as i:
                        for j in range(2):
                            ffn_act(i, j)
                    ffn_act(KFH // 2, 0)
                end_layer(act, lay)
            norm_squares(0, None)
            norm_root(0)

        @block.vector
        def _(dve):
            V = nc.vector

            def norm_apply(waits, rwait):
                dve.wait_ge(s_rt, rwait)
                V.reciprocal(rstd[:, :], rstd[:, :])
                dve.drain()

                def low(k):
                    dve.wait_ge(s_hi, waits + k + 1)
                    V.tensor_tensor(hlo[:, k, :], hf[k % 2][:, :], hhi[:, k, :], ALU.subtract).then_inc(s_h, 1)

                for k in range(KD):
                    if k >= 2:
                        dve.wait_ge(s_hi, waits + k - 1)
                    V.tensor_tensor(tn[k % 2][:, :], x[:, k, :], rstd[:, :], ALU.mult).then_inc(s_t, 1)
                    if k >= 1:
                        low(k - 1)
                low(KD - 1)

            for n in range(2 * NT):
                i, g = n // 2, n % 2
                dve.wait_ge(s_xT, n + 1)
                V.tensor_copy(x[:, 4 * g:4 * g + 4, i * 128:(i + 1) * 128],
                              PS[:, n % 8, :].rearrange("p (c n) -> p c n", c=4)).then_inc(s_xev, 1)
            dve.wait_ge(s_csig, 1)
            V.tensor_tensor(cs[:, :, :], cin[:, :, :], csig[:, :, :], ALU.mult).then_inc(s_cs, 1)

            with dve.Fori(0, DEPTH) as lay:
                dve.wait_ge(s_par, 16 * 14)
                for n in range(2):
                    dve.wait_ge(s_fmm, n + 1)
                    V.tensor_scalar(halves(farg[:, :]), PS[0:HID, 0:2, 0:HALF], fvec[:, n:n + 1],
                                    fvec[:, 2:3], ALU.add, ALU.mult)
                    dve.drain()
                    V.tensor_scalar(fk[:, :], farg[:, :], 1.0 / (2 * math.pi), MAGIC, ALU.mult, ALU.add)
                    dve.drain()
                    V.tensor_scalar(fk[:, :], fk[:, :], -MAGIC, None, ALU.add)
                    dve.drain()
                    for c in TWO_PI:
                        ins = V.scalar_tensor_tensor(farg[:, :], fk[:, :], -c, farg[:, :], ALU.mult, ALU.add)
                        dve.drain()
                    V.tensor_scalar(farg[:, :], farg[:, :], PI_BELOW, -PI_BELOW, ALU.min,
                                    ALU.max).then_inc(s_farg, 1)
                for n in range(4 * NT):
                    i, q = n // 4, n % 4
                    dve.wait_ge(s_hmm, n + 1)
                    V.tensor_tensor(hfull[:, i, q, :], PS[:, n % 4, :], decay[:, i, :],
                                    ALU.mult).then_inc(s_hev, 1)
                dve.drain()
                V.memset(hfull[0:1, 0:2, 1:4:2, :], 0.0)
                dve.drain()

                def even_odd(o):
                    for i in range(NT):
                        V.tensor_tensor(heo[:, i, 0, :], hfull[:, i, 2 * o, :], hfull[:, i, 2 * o + 1, :], ALU.add)
                        ins = V.tensor_tensor(heo[:, i, 1, :], hfull[:, i, 2 * o, :], hfull[:, i, 2 * o + 1, :],
                                              ALU.subtract)
                    ins.then_inc(s_heo, 1)

                even_odd(0)
                for q, i in ((0, 0), (1, 1)):
                    V.scalar_tensor_tensor(habs[:, q], hfull[:, i], -1.0, hfull[:, i], ALU.mult, ALU.max)
                for i in range(2, NT):
                    for q in range(4):
                        dve.drain()
                        V.scalar_tensor_tensor(habst[:, :], hfull[:, i, q], -1.0, hfull[:, i, q], ALU.mult, ALU.max)
                        dve.drain()
                        ins = V.tensor_tensor(habs[:, 1, q], habst[:, :], habs[:, 1, q], ALU.add)
                ins.then_inc(s_l1in, 1)
                dve.wait_ge(s_l1, 1)
                V.reciprocal(linv[:, :], PS[:, 6, 0:16])
                dve.wait_ge(s_sp, 12)
                even_odd(1)
                dve.wait_ge(s_mod, 1)
                V.tensor_tensor(mod[:, :, :], PS[:, 7, 0:96].rearrange("p (m s) -> p m s", s=2),
                                par[:, P_BADA:P_BADA + 48].unsqueeze(2).broadcast_to([128, 48, 2]), ALU.add)
                dve.drain()
                for w in range(2):
                    g = par[:, P_NMIX + 8 * w:P_NMIX + 8 * w + 8].unsqueeze(2).broadcast_to([128, KD, 2])
                    ins = V.scalar_tensor_tensor(amod[:, w], mod[:, 24 * w + 8:24 * w + 16, :], 1.0, g,
                                                 ALU.add, ALU.mult)
                ins.then_inc(s_modr, 1)
                norm_apply(0, 1)
                for n in range(12):
                    dve.wait_ge(s_uraw, n + 1 + 4)
                    r, u = rawu[n % 2], uhy[:, n, 0:T + 1]
                    V.tensor_scalar(u, r[:, 1:T + 2], par[:, P_CW + 12 + n:P_CW + 13 + n],
                                    par[:, P_CB + n:P_CB + n + 1], ALU.mult, ALU.add)
                    dve.drain()
                    V.scalar_tensor_tensor(u, r[:, 0:T + 1], par[:, P_CW + n:P_CW + n + 1], u, ALU.mult, ALU.add)
                    dve.drain()
                    V.scalar_tensor_tensor(u, r[:, 2:T + 3], par[:, P_CW + 24 + n:P_CW + 25 + n], u,
                                           ALU.mult, ALU.add).then_inc(s_uconv, 1)
                for o in range(2):
                    for s, fc in enumerate(FC_ORDER):
                        u = 5 * o + s
                        dve.wait_ge(s_z, u + 1)
                        dve.wait_ge(s_hld[u % 2], 16 * (u // 2 + 1))
                        dve.drain()
                        zr, zs = PS[:, 2 * (s % 2), :], PS[:, 2 * (s % 2) + 1, :]
                        h = hld[u % 2]
                        for t, (z, part) in enumerate(((zr, 0), (zs, 1), (zr, 1), (zs, 2 if fc < 2 else 0))):
                            V.tensor_tensor(yt[:, t, :], z, h[:, part, :], ALU.mult)
                        dve.drain()
                        V.tensor_tensor(yr[s % 2][:, 0, :], yt[:, 0, :], yt[:, 1, :], ALU.subtract)
                        V.tensor_tensor(yr[s % 2][:, 1, :], yt[:, 2, :], yt[:, 3, :], ALU.add).then_inc(s_y, 1)
                    for c in range(KB):
                        t = ztmp[c % 2]
                        dve.wait_ge(s_zb, 4 * o + c + 1)
                        dve.wait_ge(s_inv, 5 * o + 5)
                        V.scalar_tensor_tensor(t[:, 0:C], PS[:, 2, c * 128:(c + 1) * 128],
                                               linv[:, 8 * o + c:8 * o + c + 1], t[:, 0:C], ALU.mult, ALU.add)
                        V.scalar_tensor_tensor(t[:, LAT0:LAT0 + L], PS[:, 4 + c, :],
                                               linv[:, 8 * o + 4 + c:8 * o + 5 + c], t[:, LAT0:LAT0 + L],
                                               ALU.mult, ALU.add)
                        dve.drain()
                        dst = uhy[:, c, 0:T + 1] if o == 0 else t[:, 0:T + 1]
                        V.tensor_tensor(dst, t[:, 0:T + 1], uhy[:, 4 + 4 * o + c, 0:T + 1],
                                        ALU.mult).then_inc(s_zn, 1)
                        if o == 1:
                            dve.wait_ge(s_yhi, c + 1)
                            V.tensor_tensor(yhy_lo[:, c, 0:C], t[:, 0:C], yhy_hi[:, c, 0:C], ALU.subtract)
                            V.tensor_tensor(blocks_of(yhy_lo[:, c, C:T]), grid(t[:, LAT0:LAT0 + L]),
                                            blocks_of(yhy_hi[:, c, C:T]), ALU.subtract).then_inc(s_yhy, 1)
                V.memset(bexp[:, :, 0:5:4, :], 0.0)
                dve.wait_ge(s_ncache, 48)
                for d in range(3):
                    for h in range(HEADS):
                        off = 16 * d
                        src = rpbr[:, h, off:off + 7 * 31 + 16]
                        V.tensor_copy(bexp[:, h, 1 + d, :].rearrange("p (r c) -> p r c", r=ROWS),
                                      grid_rows(src))
                dve.drain()

                def na_max(n):
                    qb, h = n // HEADS, n % HEADS
                    dve.wait_ge(s_ns, n + 1)
                    m = mx[:, n % 2:n % 2 + 1]
                    if n >= 2:
                        dve.wait_ge(s_np, n - 1)
                    if qb == 0:
                        V.tensor_reduce(m, PS[:, n % 2, 0:128], AX, ALU.max)
                    else:
                        if n >= 2:
                            dve.wait_ge(s_nt, n - 1)
                        j = qb - 1
                        nk = len(NA_BLOCKS[j]) + 1
                        V.tensor_tensor_reduce(nap[n % 2][:, 0:nk * 128], PS[:, n % 2, 0:nk * 128],
                                               bexp[:, h, NA_BIAS0[j]:NA_BIAS0[j] + nk, :].rearrange("p b n -> p (b n)"),
                                               1.0, -3e38, ALU.add, ALU.max, m)
                    dve.drain()
                    V.tensor_scalar(nmx[:, n % 2:n % 2 + 1], m, -1.0, None, ALU.mult).then_inc(s_nm, 1)

                def na_keep(n):
                    qb = n // HEADS
                    nk = 1 if qb == 0 else len(NA_BLOCKS[qb - 1]) + 1
                    dve.wait_ge(s_nt, n + 1)
                    if n >= 2:
                        dve.wait_ge(s_npv, n - 1)
                    V.tensor_copy(napt[n % 2][:, 0:nk, :].rearrange("p b n -> p (b n)"),
                                  PS[:, 2 + n % 2, 0:nk * 128]).then_inc(s_npt, 1)

                def na_out(qb):
                    dve.wait_ge(s_npv, 8 * qb + 8)
                    V.reciprocal(rsum[:, 0, 8 * qb:8 * qb + 8], sums[:, 0, 8 * qb:8 * qb + 8])
                    dve.drain()
                    V.tensor_tensor(nao[:, qb, :].rearrange("p (h d) -> p h d", h=HEADS),
                                    PS[:, 4 + qb % 2, :].rearrange("p (h d) -> p h d", h=HEADS),
                                    rsum[:, 0, 8 * qb:8 * qb + 8].unsqueeze(2).broadcast_to([128, HEADS, 64]),
                                    ALU.mult).then_inc(s_no, 1)

                for n in range(40):
                    na_max(n)
                    if n >= 1:
                        na_keep(n - 1)
                    if n >= 8 and n % 8 == 2:
                        na_out(n // 8 - 1)
                na_keep(39)
                na_out(4)
                for qb in range(NT):
                    dve.wait_ge(s_nyhi, qb + 1)
                    cols = slice(qb * 128, (qb + 1) * 128)
                    V.tensor_tensor(yna_lo[:, :, cols], PS[:, 6 + qb % 2, :].rearrange("p (c n) -> p c n", c=KB),
                                    yna_hi[:, :, cols], ALU.subtract).then_inc(s_yna, 1)
                lam4 = rep[:, R_LAM:R_LAM + 128].rearrange("p (a d) -> p a d", a=4)
                for d in range(2):
                    V.tensor_tensor(lamt[:, 32 * d:32 * d + 32], lam4[:, 2 * d, :], lam4[:, 2 * d + 1, :], ALU.mult)
                dve.drain()
                V.tensor_reduce(lamt[:, 64:66], lamt[:, 0:64].rearrange("p (a d) -> p a d", a=2), AX,
                                ALU.add).then_inc(s_lamv, 1)
                dve.wait_ge(s_lame, 1)
                V.scalar_tensor_tensor(lamt[:, 68:69], lamt[:, 67:68], rep[:, R_LI:R_LI + 1], lamt[:, 66:67],
                                       ALU.subtract, ALU.subtract)
                for n in range(8):
                    dst, r = (daq, daq, daq, daq, dak, dak, dak, dak)[n], draw[n % 2]
                    dve.wait_ge(s_dqe, n + 1 + 4)
                    dve.drain()
                    V.stream_shuffle(dsw[:, :], r[:, C:T], [i ^ 1 for i in range(32)])
                    V.tensor_copy(dst[:, n % 4, 0:C], r[:, 0:C])
                    V.tensor_tensor(dst[:, n % 4, C:T], r[:, C:T], ropec[:, :], ALU.mult)
                    dve.drain()
                    V.tensor_tensor(dsw[:, :], dsw[:, :], ropes[:, :], ALU.mult)
                    dve.drain()
                    V.tensor_tensor(dst[:, n % 4, C:T], dst[:, n % 4, C:T], dsw[:, :], ALU.add).then_inc(s_drope, 1)

                dve.drain()
                for m in range(2):
                    ins = V.tensor_scalar(dkz[:, m], dak[:, :, 0:C], wcol[:, W_M0 + m:W_M0 + m + 1], None, ALU.mult)
                ins.then_inc(s_dkz, 1)

                def da_max(n):
                    qb, b, q = n // HEADS, 3 * (n % 2), 2 * (n % 2)
                    dve.wait_ge(s_ds, n + 1)
                    lo1, hi2 = (0, 640) if qb else (512, 128)
                    V.tensor_reduce(mx[:, q:q + 1], PSF[:, 512 * b + lo1:512 * b + 640], AX, ALU.max)
                    V.tensor_reduce(mx[:, q + 1:q + 2],
                                    PSF[:, 512 * (b + 1) + 384:512 * (b + 1) + 384 + hi2], AX, ALU.max)
                    dve.drain()
                    V.tensor_scalar(nmx[:, q:q + 2], mx[:, q:q + 2], -DA_SCALE, None, ALU.mult).then_inc(s_dm, 1)

                def da_diff(n):
                    qb, q = n // HEADS, 2 * (n % 2)
                    dve.wait_ge(s_dp, n + 1)
                    V.reciprocal(coef[:, q:q + 1], sums[:, 1, n:n + 1])
                    dve.drain()
                    V.scalar_tensor_tensor(coef[:, q + 1:q + 2], sums[:, 0, n:n + 1], coef[:, q:q + 1],
                                           lamt[:, 68:69], ALU.mult, ALU.mult)
                    dve.drain()
                    p1, p2 = dp1[n % 2], dp2[n % 2]
                    if qb:
                        V.scalar_tensor_tensor(p1[:, 0:512], p2[:, 128:640], coef[:, q + 1:q + 2], p1[:, 0:512],
                                               ALU.mult, ALU.add)
                    V.scalar_tensor_tensor(p1[:, 512:640], p2[:, 0:128], coef[:, q + 1:q + 2], p1[:, 512:640],
                                           ALU.mult, ALU.add).then_inc(s_da, 1)

                def da_out(qb):
                    dve.wait_ge(s_dpv, 8 * qb + 8)
                    V.reciprocal(rsum[:, 0, 8 * qb:8 * qb + 8], sums[:, 0, 8 * qb:8 * qb + 8])
                    dve.drain()
                    V.tensor_tensor(dao[:, qb, :].rearrange("p (h d) -> p h d", h=HEADS),
                                    PS[:, 7, :].rearrange("p (h d) -> p h d", h=HEADS),
                                    rsum[:, 0, 8 * qb:8 * qb + 8].unsqueeze(2).broadcast_to([128, HEADS, 64]),
                                    ALU.mult).then_inc(s_do, 1)

                dve.drain()
                da_max(0)
                for n in range(40):
                    if n + 1 < 40:
                        da_max(n + 1)
                    if n >= 8 and n % 8 == 0:
                        pass
                    da_diff(n)
                    if n >= 8 and n % 8 == 1:
                        da_out(n // 8 - 1)
                da_out(4)
                dve.drain()
                V.tensor_tensor(dosq[:, :, :], dao[:, :, :], dao[:, :, :], ALU.mult)
                dve.drain()
                V.tensor_reduce(ssq[:, :], dosq[:, :, :].rearrange("p t (h d) -> p (t h) d", h=HEADS), AX,
                                ALU.add).then_inc(s_dss, 1)
                dve.wait_ge(s_dsr, 1)
                V.reciprocal(ssq[:, :], ssq[:, :])
                V.tensor_scalar(lamt[:, 0:64], rep[:, R_SUB:R_SUB + 64], rep[:, R_LI + 1:R_LI + 2], None, ALU.mult)
                dve.drain()
                o3 = dao[:, :, :].rearrange("p t (h d) -> p (t h) d", h=HEADS)
                V.tensor_tensor(o3, o3, ssq[:, :].unsqueeze(2).broadcast_to([128, 40, 64]), ALU.mult)
                dve.drain()
                V.tensor_tensor(o3, o3, lamt[:, 0:64].unsqueeze(1).broadcast_to([128, 40, 64]),
                                ALU.mult).then_inc(s_don, 1)
                for qb in range(NT):
                    dve.wait_ge(s_dyhi, qb + 1)
                    cols = slice(qb * 128, (qb + 1) * 128)
                    V.tensor_tensor(yda_lo[:, :, cols], PS[:, qb % 2, :].rearrange("p (c n) -> p c n", c=KB),
                                    yda_hi[:, :, cols], ALU.subtract).then_inc(s_yda, 1)
                with dve.Fori(0, 4) as i:
                    for b in range(3):
                        for m in range(2):
                            g = i * 6 + b * 2 + m
                            if b == 0:
                                dve.drain()
                            dve.wait_ge(s_lift, g + 1)
                            dve.wait_ge(s_sig, g + 1 + 2)
                            if b == 0:
                                ins = V.tensor_tensor(halves(macc[m][:, :]), halves(sig[m][:, :]), pair(m), ALU.mult)
                            else:
                                ins = V.tensor_tensor(halves(sig[m][:, :]), halves(sig[m][:, :]), pair(m), ALU.mult)
                                dve.drain()
                                ins = V.tensor_tensor(macc[m][:, :], macc[m][:, :], sig[m][:, :], ALU.add)
                            ins.then_inc(s_lused, 1)
                            if b == 2:
                                dve.drain().then_inc(s_macc, 1)
                    for m in range(2):
                        dve.wait_ge(s_mhi, i * 2 + m + 1)
                        V.tensor_tensor(mglo[:, 2 * i + m, :], macc[m][:, :], mghi[:, 2 * i + m, :],
                                        ALU.subtract).then_inc(s_mg, 1)

                def add_to_x(m, p, gate, done):
                    p0, p1 = PS[:, 2 * p, :], PS[:, 2 * p + 1, :]
                    for src, cols, sgm in ((p0[:, 0:C], slice(0, C), 0), (p0[:, C:HALF], slice(C, HALF), 1),
                                           (p1[:, 0:HALF], slice(HALF, T), 1)):
                        ins = V.scalar_tensor_tensor(x[:, m, cols], src, mod[:, gate + m, sgm:sgm + 1],
                                                     x[:, m, cols], ALU.mult, ALU.add)
                    ins.then_inc(done, 1)

                for m in range(KD):
                    dve.wait_ge(s_o, m + 1)
                    add_to_x(m, m % 4, 16, s_x)
                dve.drain().then_inc(s_merged_free, 1)
                norm_apply(8, 2)
                for f in range(2):
                    def ffn_mul(i, j):
                        c = f * KFH + i * 2 + j
                        dve.drain()
                        dve.wait_ge(s_silu, c + 1)
                        V.tensor_tensor(halves(gact[j][:, :]), halves(silu[j][:, :]), pair(2 * j + 1),
                                        ALU.mult).then_inc(s_gact, 1)
                        dve.wait_ge(s_ahi, c + 1)
                        V.tensor_tensor(alo[:, i * 2 + j, :], gact[j][:, :], ahi[:, i * 2 + j, :],
                                        ALU.subtract).then_inc(s_act, 1)

                    with dve.Fori(0, KFH // 2) as i:
                        for j in range(2):
                            ffn_mul(i, j)
                    ffn_mul(KFH // 2, 0)
                    for m in range(KD):
                        dve.wait_ge(s_f, f * 8 + m + 1)
                        add_to_x(m, m % 4, 40, s_xf)
                end_layer(dve, lay, clears=True)
            dve.wait_ge(s_rt, 1)
            V.reciprocal(rstd[:, :], rstd[:, :])
            dve.drain()
            for k in range(KD):
                V.scalar_tensor_tensor(xo[:, k, :], x[:, k, :], nfin[:, k:k + 1], rstd[:, :],
                                       ALU.mult, ALU.mult).then_inc(s_xo, 1)
            for n in range(2 * NT):
                i, g = n // 2, n % 2
                dve.wait_ge(s_yT, n + 1)
                V.tensor_copy(yo[:, i, g * 512:(g + 1) * 512], PS[:, 2 + n % 6, :]).then_inc(s_yo, 1)

        @block.sync
        def _(sp):
            for n in range(2 * NT):
                i, g = n // 2, n % 2
                sp.wait_ge(s_yo, n + 1)
                sp.dma_start(a["y"][:, i, g * 512:(g + 1) * 512], yo[:, i, g * 512:(g + 1) * 512]).then_inc(s_out, 16)
            sp.wait_ge(s_out, 16 * 10)


SPECTRA = [("A", 0), ("B", 0), ("alt", 0), ("A", 1), ("B", 1), ("alt", 1),
           ("A", 2), ("B", 2), ("A", 3), ("B", 3), ("A", 4), ("B", 4)]
FC_ORDER = [1, 2, 3, 4, 0]
MAGIC = 1.5 * 2.0 ** 23


def _two_pi_parts():
    rest, parts = 2 * math.pi, []
    for bits in (10, 10):
        scale = 2.0 ** (bits - math.ceil(math.log2(rest)))
        part = math.floor(rest * scale) / scale
        parts.append(part)
        rest -= part
    return parts + [float(np.float32(rest))]


TWO_PI = _two_pi_parts()
PI_BELOW = float(np.nextafter(np.float32(math.pi), np.float32(0)))


def grid_rows(src):
    return bass.AP(src.tensor, src.offset, [list(src.ap[0]), [31, ROWS], [1, BLK]])


TOKENS = np.arange(L).reshape(ROWS, 4, BLK).transpose(1, 0, 2).reshape(-1)


def constants():
    f = np.float32
    n = {}
    n["ident"] = np.eye(128, dtype=f)
    n["ones"] = np.ones((128, 128), f)

    def tables(size):
        k = np.arange(size)
        ang = np.pi * ((k[:, None] * k[None, :]) % (2 * size)) / size
        cos, sin = np.cos(ang).astype(f), np.sin(ang).astype(f)
        fwd, inv = sin.copy(), sin.copy()
        fwd[:, 0] = inv[0, :] = 1 - 2 * (k % 2)
        return cos, fwd, inv

    for name, m in zip(("ctab", "stab", "sinv"), tables(L)):
        n[name] = np.ascontiguousarray(m.reshape(4, 128, L).transpose(1, 0, 2))
    for name, m in zip(("cctab", "cstab", "csinv"), tables(C)):
        n[name] = m
    feats, decays = [], []
    for size in (C, L):
        pos = np.arange(size, dtype=f)
        t = pos / f(size)
        bands = np.linspace(1e-4, 15, 16).astype(f)
        ang = f(2 * math.pi / size) * pos[:, None] * bands[None, :]
        feats.append(np.concatenate([t[:, None], np.cos(ang), -np.sin(ang)], axis=-1).astype(f))
        deltas = np.linspace(math.log(1e-2) / 1.5, math.log(1e-2) / 0.3, BW).astype(f)
        decays.append(np.exp(-t[:, None] * np.abs(deltas)[None, :]).astype(f))
    n["feats"] = np.ascontiguousarray(np.concatenate(feats).T)
    n["decay"] = np.ascontiguousarray(np.concatenate(decays).reshape(NT, 128, BW).transpose(1, 0, 2))
    wc = np.zeros((128, W_END), f)
    for col, size in ((W_LA, L), (W_CA, C)):
        wc[:, col] = wc[:, col + 1] = 1.0 / size
        wc[0, col], wc[0, col + 1] = 0.5 / size, 0.0
    wc[:, W_EPS] = EPS
    for m in range(2):
        wc[:, W_M0 + m] = (np.arange(128) // 32) % 2 == m
    n["wcol"] = wc
    pos = np.arange(L)[TOKENS]
    inv = (10000.0 ** (-np.arange(8, dtype=f) / 8)).astype(f)
    ang = np.concatenate([(pos // GW).astype(f)[:, None] * inv, (pos % GW).astype(f)[:, None] * inv], axis=-1)
    p = np.arange(128)
    n["ropec"] = np.ascontiguousarray(np.cos(ang).astype(f)[:, (p % 32) // 2].T)
    sign = np.where(p % 2 == 0, -1.0, 1.0).astype(f)
    n["ropes"] = np.ascontiguousarray((np.sin(ang).astype(f)[:, (p % 32) // 2] * sign).T)
    col = lambda b: BLK * b + np.arange(128) % BLK
    mask = np.zeros((128, 10, 128), f)
    for j, blocks in enumerate(NA_BLOCKS):
        cq = col(j)
        c0 = np.clip(cq - BLK // 2, 0, GW - BLK)
        for r, b in enumerate(blocks):
            ck = col(b)
            ok = (ck[None, :] >= c0[:, None]) & (ck[None, :] < c0[:, None] + BLK)
            mask[:, MASK0[j] + r, :] = np.where(ok, 0.0, NEG)
    n["maskb"] = mask
    li = [0.8 - 0.6 * math.exp(-0.3 * l) for l in range(DEPTH)]
    return n, li


def kernel(**inputs):
    import ml_dtypes
    import concourse.bacc as bacc
    from concourse import mybir as mb
    from concourse.bass_utils import run_bass_kernel_spmd

    g = {k: np.asarray(v) for k, v in inputs.items()}
    n, li = constants()
    for name in ("maskb",):
        n[name] = n[name].astype(ml_dtypes.bfloat16)
    n["identb"] = n["ident"].astype(ml_dtypes.bfloat16)

    def chunks(v):
        v = v.reshape(v.shape[:-1] + (-1, 128))
        return np.moveaxis(v, -1, 0).reshape(128, -1)

    def cols(w, c0, k=KD):
        return w[:, c0:c0 + 128].reshape(k, 128, 128).transpose(1, 0, 2).reshape(128, -1)

    strips, adas = [], []
    for l in range(DEPTH):
        wi, wl, wo, wf, wg = (g[k][l] for k in ("w_in", "w_lift", "w_out", "w_ffn_in", "w_ffn_out"))
        adas += [cols(g["w_ada"][l], 128 * m) for m in range(N_ADA)]
        strips += [cols(wi, 128 * m) for m in range(12)]
        for b in (1536, 3072):
            strips += [cols(wi, b + 128 * m) for m in range(8)]
            for s in range(4):
                v = wi[256 * s:256 * s + 256, b + 1024:b + 1536].reshape(2, 128, 512)
                strips.append(v.transpose(1, 0, 2).reshape(128, -1))
        for mp in range(4):
            for b in range(3):
                strips.append(np.concatenate([cols(wl[b], 128 * (2 * mp + m), KB) for m in range(2)], axis=1))
                strips += [cols(wi, 4608 + b * D + 128 * (2 * mp + m)) for m in range(2)]
        strips += [cols(wo, 128 * m) for m in range(8)]
        for f in range(2):
            for j in range(KFH):
                c0 = 128 * (f * KFH + j)
                strips += [cols(wf, c0), cols(wf, DFF + c0)]
            rows = wg[f * KFH * 128:(f + 1) * KFH * 128].reshape(KFH, 128, KD, 128)
            tiles = rows.transpose(2, 0, 1, 3).reshape(N_FOUT, KD, 128, 128)
            strips += [t.transpose(1, 0, 2).reshape(128, -1) for t in tiles]
    n["w_strips"] = np.stack(strips)
    n["w_ada"] = np.stack(adas)
    tok = np.concatenate([g["x_prompt"][0], g["x_sample"][0][TOKENS]])
    n["x_in"] = tok.reshape(NT, 128, D).transpose(1, 0, 2)
    n["cond"] = np.stack([g["c_ctx"], g["c"][0]], -1).reshape(KD, 128, 2).transpose(1, 0, 2)
    n["nfin"] = chunks(g["norm_final"])
    n["par"] = np.stack([np.concatenate([chunks(g[k][l]) for k in (
        "b_ada", "norm_mix", "norm_ffn", "hy_conv_w", "hy_conv_b", "hy_bias")], axis=1) for l in range(DEPTH)])
    n["rep"] = np.stack([np.concatenate([
        np.broadcast_to(v.reshape(1, -1), (128, v.size)) for v in (
            g["da_subln"][l], g["da_lambda"][l], np.array([li[l], 1 - li[l]], np.float32))], axis=1)
        for l in range(DEPTH)])
    n["fw1"], n["fw2"] = g["hy_filt_w1"], g["hy_filt_w2"]
    n["fw3"] = g["hy_filt_w3"].reshape(DEPTH, HID, 4, BW)
    n["fvec"] = np.stack([g["hy_filt_b1"], g["hy_filt_b2"], g["hy_filt_freq"]], -1)
    for k in ("cache_na_k", "cache_na_v", "cache_da_k", "cache_da_v"):
        n[k] = g[k][0].reshape(DEPTH, 128, BW)
    flat = g["na_rpb"].reshape(DEPTH, HEADS, 15 * 31)
    flat = np.pad(flat, ((0, 0), (0, 0), (32, 64)))
    p = np.arange(128)
    start = 32 + (7 - p // BLK) * 31 + 15 - p % BLK - BLK
    n["rpb"] = flat[:, :, start[:, None] + np.arange(7 * 31 + 48)[None, :]].transpose(0, 2, 1, 3)

    outs = {"y": (128, NT, D)}
    for k in ("new_na_k", "new_na_v", "new_da_k", "new_da_v"):
        outs[k] = (DEPTH, 128, BW)
    nc = bacc.Bacc("TRN2", target_bir_lowering=False, num_devices=1)
    arrays, aps = {}, {}
    for k, v in n.items():
        v = np.ascontiguousarray(v)
        arrays[f"in_{k}"] = v
        aps[k] = nc.dram_tensor(f"in_{k}", v.shape, mb.dt.from_np(v.dtype), kind="ExternalInput").ap()
    for k, s in outs.items():
        aps[k] = nc.dram_tensor(f"out_{k}", s, mb.dt.float32, kind="ExternalOutput").ap()
    build(nc, aps)
    r = run_bass_kernel_spmd(nc, [arrays], core_ids=[0]).results[0]
    y = np.asarray(r["out_y"]).transpose(1, 0, 2).reshape(T, D)
    ys = y[C:][np.argsort(TOKENS)]
    nak, nav, dak, dav = (np.asarray(r[f"out_{k}"]) for k in ("new_na_k", "new_na_v", "new_da_k", "new_da_v"))
    shape = (1, DEPTH, C, HEADS, 64)
    return (y[None, 0:C], ys[None], nak.reshape(shape), nav.reshape(shape), dak.reshape(shape),
            dav.reshape(shape))
```

```python
import math
from contextlib import ExitStack

import numpy as np
import concourse.bass as bass
from concourse import mybir

F32 = mybir.dt.float32
F32R = mybir.dt.float32r
BF16 = mybir.dt.bfloat16
ALU = mybir.AluOpType
ACT = mybir.ActivationFunctionType
AX = mybir.AxisListType.X

DEPTH = 2
D = 1024
KD = D // 128
C = 128
L = 512
T = C + L
HALF = T // 2
NT = T // 128
BW = 512
KB = BW // 128
HEADS = 8
GW = 64
ROWS = L // GW
BLK = 16
DFF = 2816
KF = DFF // 128
KFH = KF // 2
FEAT = 33
HID = 64
EPS = 1e-6
NEG = -1e30
DA_SCALE = 32 ** -0.5
TW = T + 2
LAT0 = C + 1

N_UHY, N_NA, N_DA, N_MERGE, N_OUT = 12, 12, 12, 36, 8
N_FIN, N_FOUT = 2 * KFH, KFH
S_UHY = 0
S_NA = S_UHY + N_UHY
S_DA = S_NA + N_NA
S_MERGE = S_DA + N_DA
S_OUT = S_MERGE + N_MERGE
S_FFN = S_OUT + N_OUT
STRIPS = S_FFN + 2 * (N_FIN + N_FOUT)
N_ADA = 6 * KD
N_ADA1, N_ADA2 = 3 * KD, 5 * KD
ADA_SLOTS = (2, 4, 3)

NA_BLOCKS = [[0, 1], [0, 1, 2], [1, 2, 3], [2, 3]]
NA_BIAS0 = [2, 1, 1, 0]
MASK0 = [0, 2, 5, 8]
DA_SPANS = [((512, 640), (896, 1024)), ((0, 640), (896, 1536))]

P_BADA, P_NMIX, P_NFFN, P_CW, P_CB, P_HB, P_END = 0, 48, 56, 64, 100, 112, 120
R_SUB, R_LAM, R_LI, R_END = 0, 64, 192, 194
W_LA, W_LB, W_CA, W_CB, W_EPS, W_M0, W_H0, W_END = 0, 1, 2, 3, 4, 5, 9, 11


def build(nc, a):
    ctx = ExitStack()
    with ctx:
        def sem(name):
            return ctx.enter_context(nc.semaphore(name))

        top = [-(-nc.sbuf_base // 32) * 32]

        def keep(name, shape, dt):
            size = int(np.prod(shape[1:])) * (2 if dt == BF16 else 4)
            t = nc.alloc_sbuf_tensor_at(name, list(shape), dt, offset=top[0])
            top[0] += -(-size // 32) * 32
            return t

        x = keep("x", [128, KD, T], F32)
        wraw = [keep(f"wraw{i}", [128, KD, 128], F32) for i in range(2)]
        whi = [keep(f"whi{i}", [128, KD, 128], F32R) for i in range(2)]
        wlo = [keep(f"wlo{i}", [128, KD, 128], F32R) for i in range(2)]
        ident = keep("ident", [128, 128], F32)
        identb = keep("identb", [128, 128], BF16)
        ones = keep("ones", [128, 128], F32)
        maskb = keep("maskb", [128, 10, 128], BF16)
        ropec = keep("ropec", [128, L], F32)
        ropes = keep("ropes", [128, L], F32)
        wcol = keep("wcol", [128, W_END], F32)
        par = keep("par", [128, P_END], F32)
        rep = keep("rep", [128, R_END], F32)
        nfin = keep("nfin", [128, KD], F32)
        mod = keep("mod", [128, 48, 2], F32)
        amod = keep("amod", [128, 2, KD, 2], F32)
        linv = keep("linv", [128, 16], F32)
        mraw = keep("mraw", [128, 2 * N_ADA], F32)
        mods = keep("mods", [128, DEPTH, 2 * N_ADA1], F32)
        linvs = keep("linvs", [128, DEPTH, 16], F32)
        mx = keep("mx", [128, 4], F32)
        nmx = keep("nmx", [128, 4], F32)
        sums = keep("sums", [128, 2, 40], F32)
        rsum = keep("rsum", [128, 2, 40], F32)
        sum2, rsum2 = (t[:, :, :].rearrange("p a n -> p (a n)") for t in (sums, rsum))
        coef = keep("coef", [128, 4], F32)
        lamt = keep("lamt", [128, 72], F32)
        ssq = keep("ssq", [128, 40], F32)
        base = top[0]

        def at(name, kib, shape, dt=F32):
            size = int(np.prod(shape[1:])) * (2 if dt == BF16 else 4)
            off = base + int(round(kib * 1024))
            assert off % 4 == 0 and off + size <= nc.sbuf_usable_end, (name, off + size)
            return nc.alloc_sbuf_tensor_at(name, list(shape), dt, offset=off)

        hhi = at("hhi", 0, [128, KD, T], F32R)
        hlo = at("hlo", 20, [128, KD, T], F32R)
        xin = at("xin", 0, [128, NT, D])
        hfull = at("hfull", 0, [128, NT, 4, BW])
        habs = at("habs", 40, [128, 2, 4, BW])
        heo = at("heo", 56, [128, NT, 2, BW])
        ctab = at("ctab", 76, [128, 4, L])
        stab = at("stab", 84, [128, 4, L])
        sinv = at("sinv", 92, [128, 4, L])
        cctab = at("cctab", 100, [128, C])
        cstab = at("cstab", 100.5, [128, C])
        csinv = at("csinv", 101, [128, C])
        decay = at("decay", 101.5, [128, NT, BW])
        hst = [at(f"hst{i}", 111.5 + 6 * i, [128, 3, BW]) for i in range(2)]
        feats = at("feats", 123.5, [FEAT, T])
        farg = at("farg", 126, [128, T])
        fk = at("fk", 128.5, [HID, T])
        habst = at("habst", 128.5, [128, BW])
        fw3 = at("fw3", 131, [128, 4, BW])
        fw1 = at("fw1", 139, [FEAT, HID])
        fw2 = at("fw2", 139.25, [HID, HID])
        fvec = at("fvec", 139.5, [HID, 3])
        ada = [[at(f"ada{s}{i}", k + 4 * i, [128, D]) for i in range(ADA_SLOTS[s])]
               for s, k in enumerate((140, 128.75, 136.5))]
        cond = [at(f"cond{s}", k, [128, 2, D]) for s, k in enumerate((92, 116.75, 124.5))]
        adap = [at(f"adap{s}", k, [128, D]) for s, k in enumerate((148, 124.75, 132.5))]
        csig = at("csig", 40, [128, 2, D])
        sq = [at(f"sq{i}", 40 + 2.5 * i, [128, T]) for i in range(2)]
        rstd = at("rstd", 45, [128, T])
        tn = [at(f"tn{i}", 47.5 + 2.5 * i, [128, T]) for i in range(2)]
        hf = [at(f"hf{i}", 52.5 + 2.5 * i, [128, T]) for i in range(2)]
        uhy = at("uhy", 40, [128, 12, TW])
        yhy_lo = at("yhy_lo", 40, [128, KB, T], F32R)
        zt = at("zt", 101.5, [128, NT, BW])
        yhy_hi = at("yhy_hi", 101.5, [128, KB, T], F32R)
        rawu = [at(f"rawu{i}", 111.5 + 2.625 * i, [128, TW + 2]) for i in range(2)]
        yr = [at(f"yr{i}", 116.75 + 4 * i, [128, 2, BW]) for i in range(2)]
        yt = at("yt", 124.75, [128, 4, BW])
        hld = [at(f"hld{i}", 132.75 + 6 * i, [128, 3, BW]) for i in range(2)]
        ztmp = [at(f"ztmp{i}", 144.75 + 2.625 * i, [128, TW]) for i in range(2)]
        naq = at("naq", 50.5, [128, KB, T])
        nak = at("nak", 60.5, [128, KB, T])
        yna_hi = at("yna_hi", 50.5, [128, KB, T], F32R)
        yna_lo = at("yna_lo", 60.5, [128, KB, T], F32R)
        nav = at("nav", 71, [128, NT, BW])
        nao = at("nao", 81, [128, NT, BW])
        nckt = at("nckt", 91, [128, BW])
        ncv = at("ncv", 93, [128, BW])
        nckT = at("nckT", 95, [128, KB, 128])
        nqz = [at(f"nqz{i}", 97 + i, [128, 2, 128]) for i in range(2)]
        bexp = at("bexp", 111.5, [128, HEADS, 5, 128])
        NRPB = 7 * 31 + 48
        rpbr = at("rpbr", 131.5, [128, HEADS, NRPB])
        nap = [at(f"nap{i}", 140 + 2 * i, [128, 512]) for i in range(2)]
        napt = [at(f"napt{i}", 144 + 2 * i, [128, 4, 128]) for i in range(2)]
        nkout = at("nkout", 99, [128, BW])
        daq = at("daq", 71, [128, KB, T])
        dak = at("dak", 81, [128, KB, T])
        yda_hi = at("yda_hi", 71, [128, KB, T], F32R)
        yda_lo = at("yda_lo", 81, [128, KB, T], F32R)
        dav = at("dav", 91, [128, NT, BW])
        dao = at("dao", 111.5, [128, NT, BW])
        dckt = at("dckt", 121.5, [128, BW])
        dcv = at("dcv", 123.5, [128, BW])
        dckT = at("dckT", 125.5, [128, KB, 128])
        dqz = [at(f"dqz{i}", 127.5 + 2 * i, [128, 4, 128]) for i in range(2)]
        dp1 = [at(f"dp1{i}", 133.5 + 5 * i, [128, 640]) for i in range(2)]
        dp2 = [at(f"dp2{i}", 136 + 5 * i, [128, 640]) for i in range(2)]
        dpt = [at(f"dpt{i}", 143.5 + 2.5 * i, [128, 5, 128]) for i in range(2)]
        dsw = at("dsw", 143.5, [128, L])
        draw = [at(f"draw{i}", 133.5 + 2.5 * i, [128, T]) for i in range(2)]
        dkout = at("dkout", 148.5, [128, BW])
        dosq = at("dosq", 125.5, [128, NT, BW])
        mghi = at("mghi", 111.5, [128, KD, T], F32R)
        mglo = at("mglo", 131.5, [128, KD, T], F32R)
        sig = [at(f"sig{i}", 91 + 2.5 * i, [128, T]) for i in range(2)]
        macc = [at(f"macc{i}", 96 + 2.5 * i, [128, T]) for i in range(2)]
        ahi = at("ahi", 57.5, [128, KFH, T], F32R)
        alo = at("alo", 86, [128, KFH, T], F32R)
        silu = [at(f"silu{i}", 114.5 + 2.5 * i, [128, T]) for i in range(2)]
        gact = [at(f"gact{i}", 119.5 + 2.5 * i, [128, T]) for i in range(2)]
        xo = at("xo", 57.5, [128, KD, T])
        yo = at("yo", 77.5, [128, NT, D])

        PS = ctx.enter_context(nc.psum_tensor("PS", [128, 8, 512], F32))
        PSF = PS[:, :, :].rearrange("p b n -> p (b n)")
        conds = nc.dram_tensor("conds", [128, 2, D], F32, kind="Internal").ap()
        spectra = nc.dram_tensor("spectra", [DEPTH, 2, NT, 128, 3, BW], F32, kind="Internal").ap()

        def pair(p):
            return PS[:, 2 * p:2 * p + 2, 0:HALF]

        def halves(ap):
            return ap.rearrange("p (h n) -> p h n", h=2)

        s_const = sem("consts_in")
        w_in = [sem(f"strip_in{i}") for i in range(2)]
        w_split = sem("strip_split")
        w_used = sem("strip_used")
        s_turn = sem("split_starts")
        s_sp_turn = sem("strips_start")
        s_table = sem("filter_consts_in")
        s_xT = sem("x_turned")
        s_xev = sem("x_kept")
        s_csig = sem("cond_sigmoid")
        s_cs = sem("cond_silu")
        s_csd = sem("cond_in_dram")
        s_fcleared = sem("filter_sems_cleared")
        s_cleared = sem("layer_sems_cleared")
        s_out = sem("outputs_out")
        s_filter_end = sem("filter_end")
        s_fpar = sem("filter_params_in")
        ada_in = [[sem(f"ada_in{i}") for i in range(ADA_SLOTS[0])]]
        ada_used = [sem("ada_used")]
        s_fmm = sem("filter_mlp_sum")
        s_farg = sem("filter_arg")
        s_fsin = sem("filter_sin")
        s_hmm = sem("filter_sum")
        s_hev = sem("filter_kept")
        s_l1in = sem("filter_abs")
        s_l1 = sem("filter_l1")
        s_heo = sem("filter_even_odd")
        s_sp = sem("spectrum_sum")
        s_spev = sem("spectrum_kept")
        s_spout = [sem(f"spectrum_out{i}") for i in range(2)]
        s_mods = sem("mods_kept")
        s_layer_end = sem("layer_end")
        s_par = sem("params_in")
        s_tab = sem("tables_in")
        ada_in += [[sem(f"ada_in{s}{i}") for i in range(ADA_SLOTS[s])] for s in (1, 2)]
        ada_used += [sem("ada2_used"), sem("ada3_used")]
        s_cond = sem("cond_in")
        s_modr = sem("mod_ready")
        s_sq = sem("squares")
        s_ss = sem("square_sums")
        s_rt = sem("root")
        s_rs = sem("rstd_ready")
        s_t = sem("normed")
        s_hi = sem("h_hi")
        s_h = sem("h_ready")
        s_u = sem("uhy_sum")
        s_uraw = sem("uhy_raw")
        s_uconv = sem("uhy_conv")
        s_ztm = sem("z_turned")
        s_zt = sem("zt_ready")
        s_z = sem("Z_sum")
        s_y = sem("Y_ready")
        s_hld = [sem(f"spectrum_in{i}") for i in range(2)]
        s_inv = sem("inverse_sum")
        s_zb = sem("z_bias")
        s_zn = sem("z_next")
        s_yhi = sem("yhy_hi_done")
        s_yhy = sem("yhy_done")
        s_nq = sem("na_qk_sum")
        s_nqe = sem("na_qk_kept")
        s_nv = sem("na_v_sum")
        s_nve = sem("na_v_kept")
        s_ncache = sem("na_cache_in")
        s_nct = sem("na_turned")
        s_nce = sem("na_turn_kept")
        s_bexp = sem("na_bias")
        s_nqz = sem("na_queries")
        s_ns = sem("na_scores")
        s_nm = sem("na_max")
        s_np = sem("na_probs")
        s_nt = sem("na_probs_turned")
        s_npt = sem("na_pt_ready")
        s_npv = sem("na_pv")
        s_no = sem("na_out_kept")
        s_noT = sem("na_out_turned")
        s_nyhi = sem("yna_hi_done")
        s_yna = sem("yna_done")
        s_dq = sem("da_qk_sum")
        s_dqe = sem("da_qk_raw")
        s_drope = sem("da_rope")
        s_dv = sem("da_v_sum")
        s_dve = sem("da_v_kept")
        s_dcache = sem("da_cache_in")
        s_dct = sem("da_turned")
        s_dce = sem("da_turn_kept")
        s_dqz = sem("da_queries")
        s_lamv = sem("lambda_dots")
        s_lame = sem("lambda_exp")
        s_ds = sem("da_scores")
        s_dm = sem("da_max")
        s_dp = sem("da_probs")
        s_da = sem("da_diff")
        s_dt = sem("da_diff_turned")
        s_dpt = sem("da_pt_ready")
        s_dpv = sem("da_pv")
        s_do = sem("da_out_kept")
        s_dss = sem("da_square_sums")
        s_dsr = sem("da_root")
        s_don = sem("da_out_normed")
        s_doT = sem("da_out_turned")
        s_dyhi = sem("yda_hi_done")
        s_yda = sem("yda_done")
        s_ko = sem("cache_k_out")
        s_lift = sem("lift_sum")
        s_lused = sem("lift_used")
        s_gate = sem("gate_sum")
        s_sig = sem("gate_sigmoid")
        s_macc = sem("merged")
        s_mhi = sem("merged_hi")
        s_mg = sem("merged_done")
        s_o = sem("out_sum")
        s_x = sem("x_added")
        s_fi = sem("ffn_in_sum")
        s_silu = sem("ffn_silu")
        s_gact = sem("ffn_product")
        s_ahi = sem("ffn_hi")
        s_act = sem("ffn_act")
        s_f = sem("ffn_out_sum")
        s_xf = sem("x_ffn_added")
        s_xo = sem("y_normed")
        s_yT = sem("y_turned")
        s_last = s_yo = sem("y_kept")

        filter_sems = range(s_filter_end.num, s_mods.num + 1)
        layer_sems = range(s_layer_end.num, s_last.num + 1)

        def end_filters(eng, lay, clears=False):
            eng.drain().then_inc(s_filter_end, 1)
            if clears:
                eng.wait_ge(s_filter_end, 3)
                eng.sem_clear(filter_sems)
                eng.sem_inc(s_fcleared, 1)
            eng.wait_ge(s_fcleared, lay + 1)

        def end_layer(eng, lay, clears=False):
            eng.drain().then_inc(s_layer_end, 1)
            if clears:
                eng.wait_ge(s_layer_end, 3)
                eng.sem_clear(layer_sems)
                eng.sem_inc(s_cleared, 1)
            eng.wait_ge(s_cleared, lay + 1)

        block = ctx.enter_context(nc.Block())

        def grid(ap):
            return ap.rearrange("p (r b c) -> p b r c", r=ROWS, b=4)

        def rows_of(ap):
            return ap.rearrange("p (r c) -> p r c", c=BLK)

        def blocks_of(ap):
            return ap.rearrange("p (b r c) -> p b r c", b=4, c=BLK)

        @block.sync
        def _(sp):
            for dst, src in ((xin[:, :, :], a["x_in"]), (ident[:, :], a["ident"]), (cond[0][:, :, :], a["cond"]),
                             (identb[:, :], a["identb"]), (ones[:, :], a["ones"]), (maskb[:, :, :], a["maskb"]),
                             (ropec[:, :], a["ropec"]), (ropes[:, :], a["ropes"]), (wcol[:, :], a["wcol"]),
                             (nfin[:, :], a["nfin"])):
                sp.dma_start(dst, src).then_inc(s_const, 16)
            for dst, src in ((feats[:, :], a["feats"]), (decay[:, :, :], a["decay"]),
                             (ctab[:, :, :], a["ctab"]), (stab[:, :, :], a["stab"]),
                             (cctab[:, :], a["cctab"]), (cstab[:, :], a["cstab"])):
                sp.dma_start(dst, src).then_inc(s_table, 16)
            with sp.Fori(0, DEPTH) as lay:
                for m in range(N_ADA1):
                    j = m % ADA_SLOTS[0]
                    if m >= ADA_SLOTS[0]:
                        sp.wait_ge(ada_used[0], m - ADA_SLOTS[0] + 1)
                    sp.dma_start(ada[0][j][:, :], a["w_ada"][lay, m]).then_inc(ada_in[0][j], 16)
                sp.wait_ge(s_fcleared, lay + 1)
                sp.sem_inc(s_sp_turn, 1)
            with sp.Fori(0, DEPTH) as lay:
                with sp.Fori(0, STRIPS // 2) as i:
                    for j in range(2):
                        n = lay * STRIPS + i * 2 + j
                        sp.wait_ge(w_split, n + 1)
                        sp.dma_start(wraw[j][:, :, :].rearrange("p k n -> p (k n)"),
                                     a["w_strips"][n]).then_inc(w_in[j], 16)

        @block.gpsimd
        def _(pool):
            pool.sem_inc(w_split, 2)
            with pool.Fori(0, DEPTH * STRIPS // 2) as i:
                for j in range(2):
                    pool.wait_ge(w_in[j], 16 * (i + 1))
                    pool.wait_ge(w_used, 2 * i + j + 2)
                    pool.sem_inc(s_turn, 1)
                    raw, hi, lo = (w[j][:, :, :].rearrange("p k n -> p (k n)") for w in (wraw, whi, wlo))
                    nc.gpsimd.tensor_scalar(hi, raw, 1.0, None, ALU.mult)
                    pool.drain()
                    nc.gpsimd.tensor_tensor(lo, raw, hi, ALU.subtract).then_inc(w_split, 1)

        @block.tensor
        def _(pe):
            pe.sem_inc(w_used, 2)

            def tiles_of(lay, idx, slot, work):
                pe.wait_ge(w_split, lay * STRIPS + idx + 3)
                for t, (kt, hi, lo, p, start, stop, done) in enumerate(work):
                    out = pair(p)
                    for m, (w, mv) in enumerate(((whi, hi), (whi, lo), (wlo, hi))):
                        for h in range(2):
                            ins = pe.matmul(out[:, h, :], w[slot][:, kt, :], mv[:, h * HALF:(h + 1) * HALF],
                                            start=start and m == 0, stop=stop and m == 2)
                            if t == m == h == 0:
                                ins.then_inc(w_used, 1)
                    if done is not None:
                        ins.then_inc(done, 1)

            def h_work(p, done):
                return [(k, hhi[:, k, :], hlo[:, k, :], p, k == 0, k == KD - 1,
                         done if k == KD - 1 else None) for k in range(KD)]

            def v_strips(lay, idx0, done, free):
                pe.wait_ge(*free)
                for s in range(4):
                    slot = (idx0 + s) % 2
                    pe.wait_ge(w_split, lay * STRIPS + idx0 + s + 3)
                    for kk in range(2):
                        k = 2 * s + kk
                        wv = [w[slot][:, 4 * kk:4 * kk + 4, :] for w in (whi, wlo)]
                        for i in range(NT):
                            for m, (hp, w) in enumerate(((hhi, wv[0]), (hhi, wv[1]), (hlo, wv[0]))):
                                ins = pe.matmul(PS[:, i, :], hp[:, k, i * 128:(i + 1) * 128], w,
                                                start=(k == 0 and m == 0), stop=(k == KD - 1 and m == 2))
                                if kk == i == m == 0:
                                    ins.then_inc(w_used, 1)
                ins.then_inc(done, 1)

            def norm_sums(waits):
                for k in range(KD):
                    pe.wait_ge(s_sq, waits + k + 1)
                    for h in range(2):
                        ins = pe.matmul(PS[:, h, 0:HALF], ones[:, :], sq[k % 2][:, h * HALF:(h + 1) * HALF],
                                        start=(k == 0), stop=(k == KD - 1))
                    ins.then_inc(s_ss, 1)

            pe.wait_ge(s_const, 160)
            for n in range(2 * NT):
                i, g = n // 2, n % 2
                if n >= 8:
                    pe.wait_ge(s_xev, n - 7)
                for c in range(4):
                    ins = pe.transpose(PS[:, n % 8, c * 128:(c + 1) * 128],
                                       xin[:, i, (4 * g + c) * 128:(4 * g + c + 1) * 128], ident[:, :])
                ins.then_inc(s_xT, 1)
            pe.wait_ge(s_xev, 2 * NT)

            pe.wait_ge(s_table, 16 * 6)

            with pe.Fori(0, DEPTH) as lay:
                pe.wait_ge(s_fpar, 16 * 4)
                for h in range(2):
                    ins = pe.matmul(PS[0:HID, h, 0:HALF], fw1[:, :], feats[:, h * HALF:(h + 1) * HALF],
                                    start=True, stop=True)
                ins.then_inc(s_fmm, 1)
                pe.wait_ge(s_fsin, 1)
                for h in range(2):
                    ins = pe.matmul(PS[0:HID, h, 0:HALF], fw2[:, :], farg[0:HID, h * HALF:(h + 1) * HALF],
                                    start=True, stop=True)
                ins.then_inc(s_fmm, 1)
                pe.wait_ge(s_fsin, 2)
                for n in range(4 * NT):
                    i, q = n // 4, n % 4
                    if n >= 4:
                        pe.wait_ge(s_hev, n - 3)
                    pe.matmul(PS[:, n % 4, :], farg[:, i * 128:(i + 1) * 128], fw3[:, q, :],
                              start=True, stop=True).then_inc(s_hmm, 1)
                for o in range(2):
                    if o:
                        pe.wait_ge(s_l1in, 1)
                        for r in range(2):
                            for q in range(2):
                                for c in range(KB):
                                    col = 8 * r + 4 * q + c
                                    for d in range(2):
                                        ins = pe.matmul(PS[:, 6, col:col + 1], habs[:, q, 2 * r + d, c * 128:(c + 1) * 128],
                                                        ones[:, 0:1], start=(d == 0), stop=(d == 1))
                        ins.then_inc(s_l1, 1)
                    pe.wait_ge(s_heo, o + 1)
                    for n, (kind, fc) in enumerate(SPECTRA):
                        g = 12 * o + n
                        if g >= 4:
                            pe.wait_ge(s_spev, g - 3)
                        out = PS[:, g % 4, :] if kind != "alt" else PS[0:1, g % 4, :]
                        eo = 1 if kind == "B" else 0
                        tiles = [0] if fc == 0 else [1, 2, 3, 4]
                        for r, i in enumerate(tiles):
                            if fc == 0:
                                w = {"A": cctab[:, :], "B": cstab[:, :], "alt": cstab[:, 0:1]}[kind]
                            else:
                                cols = slice((fc - 1) * 128, fc * 128) if kind != "alt" else slice(0, 1)
                                w = (ctab if kind == "A" else stab)[:, r, cols]
                            ins = pe.matmul(out, w, heo[:, i, eo, :], start=(r == 0), stop=(r == len(tiles) - 1))
                        ins.then_inc(s_sp, 1)
                end_filters(pe, lay)

            with pe.Fori(0, DEPTH) as lay:
                for s, n in ((s_uraw, 4), (s_nqe, 4), (s_dqe, 4), (s_lused, 2), (s_sig, 2), (s_gact, 2)):
                    pe.sem_inc(s, n)
                norm_sums(0)
                pe.wait_ge(s_rt, 1)

                with pe.Fori(0, N_UHY // 4) as i:
                    for j in range(4):
                        n = i * 4 + j
                        if j == 0:
                            pe.wait_ge(s_h, KD)
                        pe.wait_ge(s_uraw, n + 1)
                        tiles_of(lay, S_UHY + n, j % 2, h_work(j, s_u))

                pe.wait_ge(s_tab, 16 * 6)
                for o in range(2):
                    for i in range(NT):
                        if o == 0:
                            pe.wait_ge(s_uconv, 4)
                            if i == 0:
                                pe.wait_ge(s_uraw, 12 + 4)
                        else:
                            pe.wait_ge(s_zn, 4)
                        if i == 4:
                            pe.wait_ge(s_zt, 5 * o + 1)
                        col = 0 if i == 0 else LAT0 + (i - 1) * 128
                        for c in range(KB):
                            ins = pe.transpose(PS[:, i % 4, c * 128:(c + 1) * 128], uhy[:, c, col:col + 128],
                                               ident[:, :])
                        ins.then_inc(s_ztm, 1)
                    pe.wait_ge(s_zt, 5 * o + 5)

                    def forward(s, fc):
                        if s >= 2:
                            pe.wait_ge(s_y, 5 * o + s - 1)
                        for part, (lt, ct) in enumerate(((ctab, cctab), (stab, cstab))):
                            out = PS[:, 2 * (s % 2) + part, :]
                            if fc == 0:
                                ins = pe.matmul(out, ct[:, :], zt[:, 0, :], start=True, stop=True)
                            else:
                                for r in range(4):
                                    ins = pe.matmul(out, lt[:, r, (fc - 1) * 128:fc * 128], zt[:, 1 + r, :],
                                                    start=(r == 0), stop=(r == 3))
                        ins.then_inc(s_z, 1)

                    def inverse(s, fc):
                        pe.wait_ge(s_y, 5 * o + s + 1)
                        for c in range(KB):
                            for part, (lt, ct) in enumerate(((ctab, cctab), (sinv, csinv))):
                                w = yr[s % 2][:, part, c * 128:(c + 1) * 128]
                                if fc == 0:
                                    ins = pe.matmul(PS[:, 2, c * 128:(c + 1) * 128], w, ct[:, :],
                                                    start=(part == 0), stop=(part == 1))
                                else:
                                    ins = pe.matmul(PS[:, 4 + c, :], w, lt[:, fc - 1, :],
                                                    start=(fc == 1 and part == 0), stop=(fc == 4 and part == 1))
                            if fc == 4:
                                ins.then_inc(s_inv, 1)
                        if fc == 0:
                            ins.then_inc(s_inv, 1)

                    for s, fc in enumerate(FC_ORDER):
                        forward(s, fc)
                        if s >= 1:
                            inverse(s - 1, FC_ORDER[s - 1])
                    inverse(NT - 1, FC_ORDER[NT - 1])

                pe.wait_ge(s_yhy, 4)
                with pe.Fori(0, 2) as i:
                    for j in range(4):
                        pe.wait_ge(s_nqe, i * 4 + j + 1)
                        tiles_of(lay, S_NA + i * 4 + j, j % 2, h_work(j, s_nq))

                v_strips(lay, S_NA + 8, s_nv, (s_nqe, 12))
                pe.wait_ge(s_ncache, 48)
                for c in range(KB):
                    ins = pe.transpose(PS[:, 6, c * 128:(c + 1) * 128], nckt[:, c * 128:(c + 1) * 128], ident[:, :])
                ins.then_inc(s_nct, 1)
                for c in range(KB):
                    ins = pe.transpose(PS[:, 7, c * 128:(c + 1) * 128], nak[:, c, 0:C], ident[:, :])
                ins.then_inc(s_nct, 1)
                pe.wait_ge(s_nve, 5)
                pe.wait_ge(s_nce, 2)

                def na_scores(n):
                    qb, h = n // HEADS, n % HEADS
                    if n >= 2:
                        pe.wait_ge(s_np, n - 1)
                    pe.wait_ge(s_nqz, n // 2 + 1)
                    ch = h // 2
                    out = PS[:, n % 2, :]
                    q = nqz[n // 2 % 2][:, h % 2, :]
                    if qb == 0:
                        pe.matmul(out[:, 0:128], q, nak[:, ch, 0:C], start=True, stop=True).then_inc(s_ns, 1)
                        return
                    j = qb - 1
                    b0, nb = NA_BLOCKS[j][0], len(NA_BLOCKS[j])
                    lat0, cache0 = (128, 0) if j == 3 else (0, nb * 128)
                    lat = out[:, lat0:lat0 + nb * 128]
                    pe.matmul(lat, q, nak[:, ch, C + b0 * 128:C + (b0 + nb) * 128],
                              start=True, stop=False)
                    pe.matmul(lat, identb[:, :], maskb[:, MASK0[j]:MASK0[j] + nb, :], start=False, stop=True)
                    pe.matmul(out[:, cache0:cache0 + 128], q, nckT[:, ch, :],
                              start=True, stop=True).then_inc(s_ns, 1)

                def na_turn(n):
                    qb = n // HEADS
                    nk = 1 if qb == 0 else len(NA_BLOCKS[qb - 1]) + 1
                    pe.wait_ge(s_np, n + 1)
                    if n >= 2:
                        pe.wait_ge(s_npt, n - 1)
                    for i in range(nk):
                        ins = pe.transpose(PS[:, 2 + n % 2, i * 128:(i + 1) * 128],
                                           nap[n % 2][:, i * 128:(i + 1) * 128], ident[:, :])
                    ins.then_inc(s_nt, 1)

                def na_pv(n):
                    qb, h = n // HEADS, n % HEADS
                    pe.wait_ge(s_npt, n + 1)
                    if h == 0 and qb >= 2:
                        pe.wait_ge(s_no, qb - 1)
                    hc = slice(h * 64, (h + 1) * 64)
                    if qb == 0:
                        vs = [nav[:, 0, hc]]
                    else:
                        vs = [nav[:, 1 + b, hc] for b in NA_BLOCKS[qb - 1]]
                        vs = [ncv[:, hc]] + vs if qb == 4 else vs + [ncv[:, hc]]
                    for i, v in enumerate(vs):
                        ins = pe.matmul(PS[:, 4 + qb % 2, hc], napt[n % 2][:, i, :], v,
                                        start=(i == 0), stop=(i == len(vs) - 1))
                    ins.then_inc(s_npv, 1)

                na_scores(0)
                for n in range(40):
                    if n + 1 < 40:
                        na_scores(n + 1)
                    na_turn(n)
                    if n >= 1:
                        na_pv(n - 1)
                na_pv(39)
                for qb in range(NT):
                    pe.wait_ge(s_no, qb + 1)
                    if qb >= 2:
                        pe.wait_ge(s_yna, qb - 1)
                    for c in range(KB):
                        ins = pe.transpose(PS[:, 6 + qb % 2, c * 128:(c + 1) * 128],
                                           nao[:, qb, c * 128:(c + 1) * 128], ident[:, :])
                    ins.then_inc(s_noT, 1)

                pe.wait_ge(s_yna, 5)
                with pe.Fori(0, 2) as i:
                    for j in range(4):
                        pe.wait_ge(s_dqe, i * 4 + j + 1)
                        tiles_of(lay, S_DA + i * 4 + j, j % 2, h_work(j, s_dq))
                v_strips(lay, S_DA + 8, s_dv, (s_dqe, 12))
                pe.wait_ge(s_dcache, 32)
                for c in range(KB):
                    ins = pe.transpose(PS[:, 6, c * 128:(c + 1) * 128], dckt[:, c * 128:(c + 1) * 128], ident[:, :])
                ins.then_inc(s_dct, 1)
                pe.wait_ge(s_drope, 8)
                for c in range(KB):
                    ins = pe.transpose(PS[:, 7, c * 128:(c + 1) * 128], dak[:, c, 0:C], ident[:, :])
                ins.then_inc(s_dct, 1)
                pe.wait_ge(s_dve, 5)
                pe.wait_ge(s_dce, 2)

                def da_scores(n, first):
                    qb, ch = n // HEADS, n % HEADS // 2
                    b = 3 * (n % 2)
                    q = [dqz[n // 2 % 2][:, 2 * (n % 2) + m, :] for m in range(2)]
                    if first:
                        pe.wait_ge(s_dqz, n // 2 + 1)
                        if n >= 2:
                            pe.wait_ge(s_dp, n - 1)
                        for m in range(2):
                            ins = pe.matmul(PS[:, b + 1, 384 * m:384 * m + 128], q[m],
                                            dckT[:, ch, :] if qb else dak[:, ch, 0:C], start=True, stop=True)
                        if qb == 0:
                            ins.then_inc(s_ds, 2)
                    if qb:
                        m = 0 if first else 1
                        pe.matmul(PS[:, b + 2 * m, :], q[m], dak[:, ch, C:T], start=True, stop=True).then_inc(s_ds, 1)

                def da_turn(n):
                    pe.wait_ge(s_da, n + 1)
                    if n >= 1:
                        pe.wait_ge(s_dpt, n)
                    if n // HEADS:
                        for i in range(4):
                            pe.transpose(PS[:, 6, i * 128:(i + 1) * 128], dp1[n % 2][:, i * 128:(i + 1) * 128],
                                         ident[:, :])
                    if n >= 1:
                        pe.wait_ge(s_do, n)
                    pe.transpose(PS[:, 7, 0:128], dp1[n % 2][:, 512:640], ident[:, :]).then_inc(s_dt, 1)

                def da_pv(n):
                    qb, h = n // HEADS, n % HEADS
                    pe.wait_ge(s_dpt, n + 1)
                    hc = slice(h * 64, (h + 1) * 64)
                    vs = [(4, dav[:, 0, hc])] if qb == 0 else \
                        [(i, dav[:, 1 + i, hc]) for i in range(4)] + [(4, dcv[:, hc])]
                    for r, (i, v) in enumerate(vs):
                        ins = pe.matmul(PS[:, 7, 128:192], dpt[n % 2][:, i, :], v,
                                        start=(r == 0), stop=(r == len(vs) - 1))
                    ins.then_inc(s_dpv, 1)

                for n in range(2):
                    da_scores(n, True)
                    da_scores(n, False)
                for n in range(40):
                    if n + 2 < 40:
                        da_scores(n + 2, True)
                    da_turn(n)
                    if n + 2 < 40:
                        da_scores(n + 2, False)
                    da_pv(n)
                pe.wait_ge(s_don, 1)
                for qb in range(NT):
                    if qb >= 2:
                        pe.wait_ge(s_yda, qb - 1)
                    for c in range(KB):
                        ins = pe.transpose(PS[:, qb % 2, c * 128:(c + 1) * 128],
                                           dao[:, qb, c * 128:(c + 1) * 128], ident[:, :])
                    ins.then_inc(s_doT, 1)
                pe.wait_ge(s_yda, 5)

                ys = ((yhy_hi, yhy_lo), (yna_hi, yna_lo), (yda_hi, yda_lo))
                with pe.Fori(0, 2) as i:
                    for mp in range(2):
                        for b in range(3):
                            g = i * 12 + mp * 6 + b * 2
                            s0 = S_MERGE + i * 18 + mp * 9 + b * 3
                            sl = (mp * 9 + b * 3) % 2
                            for m in range(2):
                                pe.wait_ge(s_sig, g + m + 1)
                                tiles_of(lay, s0 + m, (sl + m) % 2, h_work(2 + m, s_gate))
                            pe.wait_ge(s_lused, g + 2)
                            tiles_of(lay, s0 + 2, sl, [
                                (4 * m + k, ys[b][0][:, k, :], ys[b][1][:, k, :], m, k == 0, k == KB - 1,
                                 s_lift if k == KB - 1 else None) for m in range(2) for k in range(KB)])

                pe.wait_ge(s_mg, 8)
                pe.wait_ge(s_sig, 26)
                for m in range(KD):
                    if m >= 4:
                        pe.wait_ge(s_x, m - 3)
                    tiles_of(lay, S_OUT + m, m % 2, [
                        (k, mghi[:, k, :], mglo[:, k, :], m % 4, k == 0, k == KD - 1,
                         s_o if k == KD - 1 else None) for k in range(KD)])

                pe.wait_ge(s_x, 8)
                norm_sums(8)
                pe.wait_ge(s_rt, 2)
                pe.wait_ge(s_h, 16)

                for f in range(2):
                    s0 = S_FFN + f * (N_FIN + N_FOUT)
                    if f:
                        pe.wait_ge(s_xf, 8)

                    def ffn_in(i, j, slot):
                        pe.wait_ge(s_gact, f * KFH + i * 2 + j + 1)
                        for u in range(2):
                            tiles_of(lay, s0 + (i * 2 + j) * 2 + u, (slot + u) % 2,
                                     h_work(2 * j + u, s_fi if u else None))

                    with pe.Fori(0, KFH // 2) as i:
                        for j in range(2):
                            ffn_in(i, j, s0 % 2)
                    ffn_in(KFH // 2, 0, s0 % 2)
                    pe.wait_ge(s_act, (f + 1) * KFH)
                    s1 = s0 + N_FIN
                    for st in range(N_FOUT):
                        work = []
                        for kt in range(KD):
                            m, k = divmod(st * KD + kt, KFH)
                            work.append((kt, ahi[:, k, :], alo[:, k, :], m % 4, k == 0, k == KFH - 1,
                                         s_f if k == KFH - 1 else None))
                        for m in range(4, KD):
                            if (m * KFH) // KD == st:
                                pe.wait_ge(s_xf, f * 8 + m - 3)
                        tiles_of(lay, s1 + st, (s1 + st) % 2, work)
                end_layer(pe, lay)

            norm_sums(0)
            for n in range(2 * NT):
                i, g = n // 2, n % 2
                pe.wait_ge(s_xo, 8 if g else 4)
                if n >= 6:
                    pe.wait_ge(s_yo, n - 5)
                for c in range(4):
                    ins = pe.transpose(PS[:, 2 + n % 6, c * 128:(c + 1) * 128],
                                       xo[:, 4 * g + c, i * 128:(i + 1) * 128], ident[:, :])
                ins.then_inc(s_yT, 1)

        @block.scalar
        def _(act):
            A = nc.scalar.activation

            def norm_squares(waits, xwait):
                for k in range(KD):
                    if xwait is not None:
                        act.wait_ge(xwait[0], xwait[1] + k + 1)
                    if k >= 2:
                        act.wait_ge(s_ss, waits + k - 1)
                    A(sq[k % 2][:, :], x[:, k, :], ACT.Square).then_inc(s_sq, 1)

            def norm_root(waits):
                act.wait_ge(s_ss, waits + KD)
                A(halves(rstd[:, :]), PS[:, 0:2, 0:HALF], ACT.Sqrt, bias=wcol[:, W_EPS:W_EPS + 1],
                  scale=1.0 / D).then_inc(s_rt, 1)

            def norm_apply(waits, which):
                shift = 24 * which
                for k in range(KD):
                    act.wait_ge(s_t, waits + k + 1)
                    if k >= 2:
                        act.wait_ge(s_h, waits + k - 1)
                    for sgm, cols in enumerate((slice(0, C), slice(C, T))):
                        A(hf[k % 2][:, cols], tn[k % 2][:, cols], ACT.Identity,
                          bias=mod[:, shift + k, sgm:sgm + 1], scale=amod[:, which, k, sgm:sgm + 1])
                    act.drain()
                    A(hhi[:, k, :], hf[k % 2][:, :], ACT.Copy).then_inc(s_hi, 1)

            act.wait_ge(s_const, 160)
            A(csig[:, :, :], cond[0][:, :, :], ACT.Sigmoid).then_inc(s_csig, 1)
            act.wait_ge(s_cs, 1)
            act.dma_start(conds, cond[0][:, :, :]).then_inc(s_csd, 16)
            act.wait_ge(s_csd, 16)
            act.wait_ge(s_xev, 2 * NT)
            with act.Fori(0, DEPTH) as lay:
                for dst, src in ((fw1[:, :], a["fw1"][lay]), (fw2[:, :], a["fw2"][lay]),
                                 (fw3[0:HID, :, :], a["fw3"][lay]), (fvec[:, :], a["fvec"][lay])):
                    act.dma_start(dst, src).then_inc(s_fpar, 16)
                for n in range(2):
                    act.wait_ge(s_farg, n + 1)
                    A(farg[0:HID, :], farg[0:HID, :], ACT.Sin).then_inc(s_fsin, 1)
                for o in range(2):
                    for n, (kind, fc) in enumerate(SPECTRA):
                        g = 12 * o + n
                        act.wait_ge(s_sp, g + 1)
                        buf = 5 * o + fc
                        st = hst[buf % 2]
                        ps = PS[:, g % 4, :]
                        seq = L if fc else C
                        if kind == "A":
                            if buf >= 2:
                                act.wait_ge(s_spout[buf % 2], 16 * (buf // 2))
                            w = wcol[:, (W_LA if fc else W_CA):(W_LA if fc else W_CA) + 1] if fc < 2 else 1.0 / L
                            ins = A(st[:, 0, :], ps, ACT.Copy, scale=w)
                            if fc < 2:
                                ins = A(st[:, 2, :], ps, ACT.Copy, scale=w)
                        elif kind == "B":
                            w = wcol[:, (W_LB if fc else W_CB):(W_LB if fc else W_CB) + 1] if fc < 2 else 1.0 / L
                            ins = A(st[:, 1, :], ps, ACT.Copy, scale=w)
                        else:
                            act.drain()
                            ins = A(st[0:1, 2, :], ps[0:1, :], ACT.Copy, scale=0.5 / seq)
                        ins.then_inc(s_spev, 1)
                        if kind == "alt" or (kind == "B" and fc >= 2):
                            parts = 3 if fc < 2 else 2
                            act.wait_ge(s_spev, g + 1)
                            act.dma_start(spectra[lay, o, fc, :, 0:parts, :], st[:, 0:parts, :]).then_inc(
                                s_spout[buf % 2], 16)
                for b in range(2):
                    act.wait_ge(s_spout[b], 16 * 5)
                end_filters(act, lay)

            def ada_load(s, n, m):
                j = n % ADA_SLOTS[s]
                if n >= ADA_SLOTS[s]:
                    act.wait_ge(ada_used[s], n - ADA_SLOTS[s] + 1)
                act.dma_start(ada[s][j][:, :], a["w_ada"][lay, m]).then_inc(ada_in[s][j], 16)

            with act.Fori(0, DEPTH) as lay:
                for dst, src in ((par[:, :], a["par"][lay]), (rep[:, :], a["rep"][lay])):
                    act.dma_start(dst, src).then_inc(s_par, 16)
                for dst, src in ((ctab[:, :, :], a["ctab"]), (stab[:, :, :], a["stab"]),
                                 (sinv[:, :, :], a["sinv"]), (cctab[:, :], a["cctab"]),
                                 (cstab[:, :], a["cstab"]), (csinv[:, :], a["csinv"])):
                    act.dma_start(dst, src).then_inc(s_tab, 16)
                act.dma_start(cond[1][:, :, :], conds).then_inc(s_cond, 16)
                norm_squares(0, None)
                norm_root(0)
                act.wait_ge(s_modr, 1)
                norm_apply(0, 0)
                for b in range(2):
                    for col in (0, LAT0, LAT0 + 1 + L):
                        nc.scalar.activation(rawu[b][:, col:col + 1], ones[:, 0:1], ACT.Copy, scale=0.0)
                act.wait_ge(s_h, 8)
                for n in range(12):
                    for k in range(0 if n == 0 else 2 * n + 2, min(2 * n + 4, N_ADA2 - N_ADA1)):
                        ada_load(1, k, N_ADA1 + k)
                    act.wait_ge(s_u, n + 1)
                    if n >= 2:
                        act.wait_ge(s_uconv, n - 1)
                    r = rawu[n % 2]
                    g = grid(r[:, LAT0 + 1:LAT0 + 1 + L])
                    p0, p1 = PS[:, 2 * (n % 4), :], PS[:, 2 * (n % 4) + 1, :]
                    A(r[:, 1:1 + C], p0[:, 0:C], ACT.Copy)
                    A(g[:, 0], rows_of(p0[:, C:C + 128]), ACT.Copy)
                    A(g[:, 1, 0:4], rows_of(p0[:, C + 128:HALF]), ACT.Copy)
                    A(g[:, 1, 4:8], rows_of(p1[:, 0:64]), ACT.Copy)
                    A(g[:, 2:4], p1[:, 64:HALF].rearrange("p (b r c) -> p b r c", b=2, c=BLK),
                      ACT.Copy).then_inc(s_uraw, 1)
                for o in range(2):
                    def load_spectrum(s):
                        fc = FC_ORDER[s]
                        parts = 3 if fc < 2 else 2
                        u = 5 * o + s
                        if u >= 2:
                            act.wait_ge(s_y, u - 1)
                        act.dma_start(hld[u % 2][:, 0:parts, :], spectra[lay, o, fc, :, 0:parts, :]).then_inc(
                            s_hld[u % 2], 16)

                    if o == 0:
                        act.wait_ge(s_modr, 2)
                    load_spectrum(0)
                    load_spectrum(1)
                    for i in range(NT):
                        act.wait_ge(s_ztm, 5 * o + i + 1)
                        A(zt[:, i, :], PS[:, i % 4, :], ACT.Copy).then_inc(s_zt, 1)
                    for s in range(2, NT):
                        load_spectrum(s)
                    for c in range(KB):
                        if c >= 2:
                            act.wait_ge(s_zn, 4 * o + c - 1)
                        if o == 0 and c == 0:
                            act.wait_ge(s_uconv, 12)
                        A(ztmp[c % 2][:, 0:T + 1], uhy[:, c, 0:T + 1], ACT.Copy,
                          scale=par[:, P_HB + 4 * o + c:P_HB + 4 * o + c + 1]).then_inc(s_zb, 1)
                        if o == 1:
                            act.wait_ge(s_zn, 4 * o + c + 1)
                            if c == 0:
                                act.wait_ge(s_z, 10)
                            A(yhy_hi[:, c, 0:C], ztmp[c % 2][:, 0:C], ACT.Copy)
                            A(blocks_of(yhy_hi[:, c, C:T]), grid(ztmp[c % 2][:, LAT0:LAT0 + L]), ACT.Copy).then_inc(s_yhi, 1)
                act.wait_ge(s_yhy, 4)
                act.dma_start(nckt[:, :], a["cache_na_k"][lay]).then_inc(s_ncache, 16)
                act.dma_start(ncv[:, :], a["cache_na_v"][lay]).then_inc(s_ncache, 16)
                act.dma_start(rpbr[:, :, :], a["rpb"][lay]).then_inc(s_ncache, 16)
                for n in range(8):
                    act.wait_ge(s_nq, n + 1)
                    dst, sc = (naq, 0.125) if n < 4 else (nak, 1.0)
                    A(halves(dst[:, n % 4, :]), pair(n % 4), ACT.Copy, scale=sc).then_inc(s_nqe, 1)
                act.wait_ge(s_nv, 1)
                for i in range(NT):
                    A(nav[:, i, :], PS[:, i, :], ACT.Copy).then_inc(s_nve, 1)
                act.wait_ge(s_nve, 1)
                act.dma_start(a["new_na_v"][lay], nav[:, 0, :]).then_inc(s_ko, 16)
                act.wait_ge(s_nct, 1)
                A(nckT[:, :, :].rearrange("p c n -> p (c n)"), PS[:, 6, :], ACT.Copy).then_inc(s_nce, 1)
                act.wait_ge(s_nct, 2)
                A(nkout[:, :], PS[:, 7, :], ACT.Copy).then_inc(s_nce, 1)
                act.wait_ge(s_nce, 2)
                act.dma_start(a["new_na_k"][lay], nkout[:, :]).then_inc(s_ko, 16)
                for n in range(40):
                    qb = n // HEADS
                    nk = 128 * (1 if qb == 0 else len(NA_BLOCKS[qb - 1]) + 1)
                    act.wait_ge(s_nm, n + 1)
                    if qb == 0 and n >= 2:
                        act.wait_ge(s_nt, n - 1)
                    src = PS[:, n % 2, 0:nk] if qb == 0 else nap[n % 2][:, 0:nk]
                    A(nap[n % 2][:, 0:nk], src, ACT.Exp, bias=nmx[:, n % 2:n % 2 + 1], scale=1.0,
                      accum_out=sums[:, 0, n:n + 1]).then_inc(s_np, 1)
                for qb in range(NT):
                    act.wait_ge(s_noT, qb + 1)
                    src = PS[:, 6 + qb % 2, :]
                    A(yna_hi[:, :, qb * 128:(qb + 1) * 128], src.rearrange("p (c n) -> p c n", c=KB),
                      ACT.Copy).then_inc(s_nyhi, 1)
                act.wait_ge(s_yna, 5)
                act.wait_ge(s_ko, 16 * 2)
                act.dma_start(dckt[:, :], a["cache_da_k"][lay]).then_inc(s_dcache, 16)
                act.dma_start(dcv[:, :], a["cache_da_v"][lay]).then_inc(s_dcache, 16)
                act.wait_ge(s_lamv, 1)
                A(lamt[:, 66:68], lamt[:, 64:66], ACT.Exp).then_inc(s_lame, 1)
                for n in range(8):
                    act.wait_ge(s_dq, n + 1)
                    if n >= 2:
                        act.wait_ge(s_drope, n - 1)
                    A(halves(draw[n % 2][:, :]), pair(n % 4), ACT.Copy).then_inc(s_dqe, 1)
                act.wait_ge(s_dv, 1)
                for i in range(NT):
                    A(dav[:, i, :], PS[:, i, :], ACT.Copy).then_inc(s_dve, 1)
                act.wait_ge(s_dve, 1)
                act.dma_start(a["new_da_v"][lay], dav[:, 0, :]).then_inc(s_ko, 16)
                act.wait_ge(s_dct, 1)
                A(dckT[:, :, :].rearrange("p c n -> p (c n)"), PS[:, 6, :], ACT.Copy).then_inc(s_dce, 1)
                act.wait_ge(s_dct, 2)
                A(dkout[:, :], PS[:, 7, :], ACT.Copy).then_inc(s_dce, 1)
                act.wait_ge(s_dce, 2)
                act.dma_start(a["new_da_k"][lay], dkout[:, :]).then_inc(s_ko, 16)

                def da_exp(n):
                    qb, b, q = n // HEADS, 3 * (n % 2), 2 * (n % 2)
                    act.wait_ge(s_dm, n + 1)
                    if n >= 2:
                        act.wait_ge(s_dt, n - 1)
                    (lo1, hi1), (lo2, hi2) = DA_SPANS[qb > 0]
                    A(dp1[n % 2][:, lo1:hi1], PSF[:, 512 * b + lo1:512 * b + hi1], ACT.Exp,
                      bias=nmx[:, q:q + 1], scale=DA_SCALE, accum_out=sum2[:, 2 * n:2 * n + 1])
                    A(dp2[n % 2][:, lo2 - 896:hi2 - 896], PSF[:, 512 * b + lo2:512 * b + hi2], ACT.Exp,
                      bias=nmx[:, q + 1:q + 2], scale=DA_SCALE,
                      accum_out=sum2[:, 2 * n + 1:2 * n + 2]).then_inc(s_dp, 1)

                def da_keep(n):
                    qb = n // HEADS
                    act.wait_ge(s_dt, n + 1)
                    if n >= 2:
                        act.wait_ge(s_dpv, n - 1)
                    lo = 0 if qb else 512
                    A(dpt[n % 2][:, :, :].rearrange("p i n -> p (i n)")[:, lo:640], PSF[:, 3072 + lo:3072 + 640],
                      ACT.Copy).then_inc(s_dpt, 1)

                da_exp(0)
                da_exp(1)
                for n in range(40):
                    da_keep(n)
                    if n + 2 < 40:
                        da_exp(n + 2)
                act.wait_ge(s_dss, 1)
                A(ssq[:, :], ssq[:, :], ACT.Sqrt, bias=wcol[:, W_EPS:W_EPS + 1],
                  scale=1.0 / 64).then_inc(s_dsr, 1)
                for qb in range(NT):
                    act.wait_ge(s_doT, qb + 1)
                    A(yda_hi[:, :, qb * 128:(qb + 1) * 128], PS[:, qb % 2, :].rearrange("p (c n) -> p c n", c=KB),
                      ACT.Copy).then_inc(s_dyhi, 1)
                act.wait_ge(s_ko, 16 * 4)
                with act.Fori(0, 4) as i:
                    for b in range(3):
                        for m in range(2):
                            g = i * 6 + b * 2 + m
                            act.wait_ge(s_gate, g + 1)
                            act.wait_ge(s_lused, g + 1)
                            A(halves(sig[m][:, :]), pair(2 + m), ACT.Sigmoid).then_inc(s_sig, 1)
                    for m in range(2):
                        act.wait_ge(s_macc, i * 2 + m + 1)
                        A(mghi[:, 2 * i + m, :], macc[m][:, :], ACT.Copy).then_inc(s_mhi, 1)
                norm_squares(8, (s_x, 0))
                act.dma_start(cond[2][:, :, :], conds).then_inc(s_cond, 16)
                for n in range(ADA_SLOTS[2]):
                    ada_load(2, n, N_ADA2 + n)
                norm_root(8)
                norm_apply(8, 1)
                for f in range(2):
                    if f:
                        act.wait_ge(s_xf, 8)

                    def ffn_act(i, j):
                        c = f * KFH + i * 2 + j
                        act.wait_ge(s_fi, c + 1)
                        act.wait_ge(s_gact, c + 1)
                        A(halves(silu[j][:, :]), pair(2 * j), ACT.Silu).then_inc(s_silu, 1)
                        act.wait_ge(s_gact, c + 3)
                        A(ahi[:, i * 2 + j, :], gact[j][:, :], ACT.Copy).then_inc(s_ahi, 1)

                    with act.Fori(0, KFH // 2) as i:
                        for j in range(2):
                            ffn_act(i, j)
                    ffn_act(KFH // 2, 0)
                    if f == 0:
                        for n in range(ADA_SLOTS[2], N_ADA - N_ADA2):
                            ada_load(2, n, N_ADA2 + n)
                end_layer(act, lay)
            norm_squares(0, None)
            norm_root(0)

        @block.vector
        def _(dve):
            V = nc.vector

            def norm_apply(waits, rwait):
                dve.wait_ge(s_rt, rwait)
                V.reciprocal(rstd[:, :], rstd[:, :])
                dve.drain()

                def low(k):
                    dve.wait_ge(s_hi, waits + k + 1)
                    V.tensor_tensor(hlo[:, k, :], hf[k % 2][:, :], hhi[:, k, :], ALU.subtract).then_inc(s_h, 1)

                for k in range(KD):
                    if k >= 2:
                        dve.wait_ge(s_hi, waits + k - 1)
                    V.tensor_tensor(tn[k % 2][:, :], x[:, k, :], rstd[:, :], ALU.mult).then_inc(s_t, 1)
                    if k >= 1:
                        low(k - 1)
                low(KD - 1)

            for n in range(2 * NT):
                i, g = n // 2, n % 2
                dve.wait_ge(s_xT, n + 1)
                V.tensor_copy(x[:, 4 * g:4 * g + 4, i * 128:(i + 1) * 128],
                              PS[:, n % 8, :].rearrange("p (c n) -> p c n", c=4)).then_inc(s_xev, 1)
            dve.wait_ge(s_csig, 1)
            V.tensor_tensor(cond[0][:, :, :], cond[0][:, :, :], csig[:, :, :], ALU.mult).then_inc(s_cs, 1)
            dve.wait_ge(s_csd, 16)

            def ada_dot(s, n, m):
                j = n % ADA_SLOTS[s]
                dve.wait_ge(ada_in[s][j], 16 * (n // ADA_SLOTS[s] + 1))
                for c in range(2):
                    dve.drain()
                    ins = V.tensor_tensor_reduce(adap[s][:, :], ada[s][j][:, :], cond[s][:, c, :], 1.0, 0.0,
                                                 ALU.mult, ALU.add, mraw[:, 2 * m + c:2 * m + c + 1])
                ins.then_inc(ada_used[s], 1)

            V.memset(farg[HID:128, :], 0.0)
            V.memset(fw3[HID:128, :, :], 0.0)
            dve.wait_ge(s_const, 160)
            dve.wait_ge(s_table, 16 * 6)

            with dve.Fori(0, DEPTH) as lay:
                dve.wait_ge(s_fpar, 16 * 4)
                for n in range(2):
                    dve.wait_ge(s_fmm, n + 1)
                    V.tensor_scalar(halves(farg[0:HID, :]), PS[0:HID, 0:2, 0:HALF], fvec[:, n:n + 1],
                                    fvec[:, 2:3], ALU.add, ALU.mult)
                    dve.drain()
                    V.tensor_scalar(fk[:, :], farg[0:HID, :], 1.0 / (2 * math.pi), MAGIC, ALU.mult, ALU.add)
                    dve.drain()
                    V.tensor_scalar(fk[:, :], fk[:, :], -MAGIC, None, ALU.add)
                    dve.drain()
                    for c in TWO_PI:
                        ins = V.scalar_tensor_tensor(farg[0:HID, :], fk[:, :], -c, farg[0:HID, :], ALU.mult, ALU.add)
                        dve.drain()
                    V.tensor_scalar(farg[0:HID, :], farg[0:HID, :], PI_BELOW, -PI_BELOW, ALU.min,
                                    ALU.max).then_inc(s_farg, 1)
                for n in range(4 * NT):
                    i, q = n // 4, n % 4
                    dve.wait_ge(s_hmm, n + 1)
                    V.tensor_tensor(hfull[:, i, q, :], PS[:, n % 4, :], decay[:, i, :],
                                    ALU.mult).then_inc(s_hev, 1)
                dve.drain()
                V.memset(hfull[0:1, 0:2, 1:4:2, :], 0.0)
                dve.drain()

                def even_odd(o):
                    for i in range(NT):
                        V.tensor_tensor(heo[:, i, 0, :], hfull[:, i, 2 * o, :], hfull[:, i, 2 * o + 1, :], ALU.add)
                        ins = V.tensor_tensor(heo[:, i, 1, :], hfull[:, i, 2 * o, :], hfull[:, i, 2 * o + 1, :],
                                              ALU.subtract)
                    ins.then_inc(s_heo, 1)

                even_odd(0)
                for q, i in ((0, 0), (1, 1)):
                    V.scalar_tensor_tensor(habs[:, q], hfull[:, i], -1.0, hfull[:, i], ALU.mult, ALU.max)
                for i in range(2, NT):
                    for q in range(4):
                        dve.drain()
                        V.scalar_tensor_tensor(habst[:, :], hfull[:, i, q], -1.0, hfull[:, i, q], ALU.mult, ALU.max)
                        dve.drain()
                        ins = V.tensor_tensor(habs[:, 1, q], habst[:, :], habs[:, 1, q], ALU.add)
                ins.then_inc(s_l1in, 1)
                for m in range(KD):
                    ada_dot(0, m, m)
                dve.wait_ge(s_sp, 12)
                even_odd(1)
                dve.wait_ge(s_l1, 1)
                V.reciprocal(linvs[:, lay], PS[:, 6, 0:16])
                for m in range(KD, N_ADA1):
                    ada_dot(0, m, m)
                dve.drain()
                V.tensor_copy(mods[:, lay], mraw[:, 0:2 * N_ADA1]).then_inc(s_mods, 1)
                end_filters(dve, lay, clears=True)

            def modulation(m0, m1, src):
                V.tensor_tensor(mod[:, m0:m1, :], src.rearrange("p (m s) -> p m s", s=2),
                                par[:, P_BADA + m0:P_BADA + m1].unsqueeze(2).broadcast_to([128, m1 - m0, 2]), ALU.add)
                dve.drain()

            def norm_scale(w):
                g = par[:, P_NMIX + 8 * w:P_NMIX + 8 * w + 8].unsqueeze(2).broadcast_to([128, KD, 2])
                V.scalar_tensor_tensor(amod[:, w], mod[:, 24 * w + 8:24 * w + 16, :], 1.0, g,
                                       ALU.add, ALU.mult).then_inc(s_modr, 1)

            with dve.Fori(0, DEPTH) as lay:
                dve.wait_ge(s_par, 16 * 2)
                V.tensor_copy(linv[:, :], linvs[:, lay])
                modulation(0, N_ADA1, mods[:, lay])
                norm_scale(0)
                norm_apply(0, 1)
                dve.wait_ge(s_cond, 16)
                for n in range(12):
                    dve.wait_ge(s_uraw, n + 1 + 4)
                    r, u = rawu[n % 2], uhy[:, n, 0:T + 1]
                    V.tensor_scalar(u, r[:, 1:T + 2], par[:, P_CW + 12 + n:P_CW + 13 + n],
                                    par[:, P_CB + n:P_CB + n + 1], ALU.mult, ALU.add)
                    dve.drain()
                    V.scalar_tensor_tensor(u, r[:, 0:T + 1], par[:, P_CW + n:P_CW + n + 1], u, ALU.mult, ALU.add)
                    dve.drain()
                    V.scalar_tensor_tensor(u, r[:, 2:T + 3], par[:, P_CW + 24 + n:P_CW + 25 + n], u,
                                           ALU.mult, ALU.add).then_inc(s_uconv, 1)
                    for k in range(2 * n, min(2 * n + 2, N_ADA2 - N_ADA1)):
                        ada_dot(1, k, N_ADA1 + k)
                dve.drain()
                modulation(N_ADA1, N_ADA2, mraw[:, 2 * N_ADA1:2 * N_ADA2])
                norm_scale(1)
                for o in range(2):
                    for s, fc in enumerate(FC_ORDER):
                        u = 5 * o + s
                        dve.wait_ge(s_z, u + 1)
                        dve.wait_ge(s_hld[u % 2], 16 * (u // 2 + 1))
                        dve.drain()
                        zr, zs = PS[:, 2 * (s % 2), :], PS[:, 2 * (s % 2) + 1, :]
                        h = hld[u % 2]
                        for t, (z, part) in enumerate(((zr, 0), (zs, 1), (zr, 1), (zs, 2 if fc < 2 else 0))):
                            V.tensor_tensor(yt[:, t, :], z, h[:, part, :], ALU.mult)
                        dve.drain()
                        V.tensor_tensor(yr[s % 2][:, 0, :], yt[:, 0, :], yt[:, 1, :], ALU.subtract)
                        V.tensor_tensor(yr[s % 2][:, 1, :], yt[:, 2, :], yt[:, 3, :], ALU.add).then_inc(s_y, 1)
                    for c in range(KB):
                        t = ztmp[c % 2]
                        dve.wait_ge(s_zb, 4 * o + c + 1)
                        dve.wait_ge(s_inv, 5 * o + 5)
                        V.scalar_tensor_tensor(t[:, 0:C], PS[:, 2, c * 128:(c + 1) * 128],
                                               linv[:, 8 * o + c:8 * o + c + 1], t[:, 0:C], ALU.mult, ALU.add)
                        V.scalar_tensor_tensor(t[:, LAT0:LAT0 + L], PS[:, 4 + c, :],
                                               linv[:, 8 * o + 4 + c:8 * o + 5 + c], t[:, LAT0:LAT0 + L],
                                               ALU.mult, ALU.add)
                        dve.drain()
                        dst = uhy[:, c, 0:T + 1] if o == 0 else t[:, 0:T + 1]
                        V.tensor_tensor(dst, t[:, 0:T + 1], uhy[:, 4 + 4 * o + c, 0:T + 1],
                                        ALU.mult).then_inc(s_zn, 1)
                        if o == 1:
                            dve.wait_ge(s_yhi, c + 1)
                            V.tensor_tensor(yhy_lo[:, c, 0:C], t[:, 0:C], yhy_hi[:, c, 0:C], ALU.subtract)
                            V.tensor_tensor(blocks_of(yhy_lo[:, c, C:T]), grid(t[:, LAT0:LAT0 + L]),
                                            blocks_of(yhy_hi[:, c, C:T]), ALU.subtract).then_inc(s_yhy, 1)
                V.memset(bexp[:, :, 0:5:4, :], 0.0)
                dve.wait_ge(s_ncache, 48)
                for d in range(3):
                    for h in range(HEADS):
                        off = 16 * d
                        src = rpbr[:, h, off:off + 7 * 31 + 16]
                        V.tensor_copy(bexp[:, h, 1 + d, :].rearrange("p (r c) -> p r c", r=ROWS),
                                      grid_rows(src))
                dve.drain()

                def na_max(n):
                    qb, h = n // HEADS, n % HEADS
                    dve.wait_ge(s_ns, n + 1)
                    m = mx[:, n % 2:n % 2 + 1]
                    if n >= 2:
                        dve.wait_ge(s_np, n - 1)
                    if qb == 0:
                        V.tensor_reduce(m, PS[:, n % 2, 0:128], AX, ALU.max)
                    else:
                        if n >= 2:
                            dve.wait_ge(s_nt, n - 1)
                        j = qb - 1
                        nk = len(NA_BLOCKS[j]) + 1
                        V.tensor_tensor_reduce(nap[n % 2][:, 0:nk * 128], PS[:, n % 2, 0:nk * 128],
                                               bexp[:, h, NA_BIAS0[j]:NA_BIAS0[j] + nk, :].rearrange("p b n -> p (b n)"),
                                               1.0, -3e38, ALU.add, ALU.max, m)
                    dve.drain()
                    V.tensor_scalar(nmx[:, n % 2:n % 2 + 1], m, -1.0, None, ALU.mult).then_inc(s_nm, 1)

                def na_keep(n):
                    qb = n // HEADS
                    nk = 1 if qb == 0 else len(NA_BLOCKS[qb - 1]) + 1
                    dve.wait_ge(s_nt, n + 1)
                    if n >= 2:
                        dve.wait_ge(s_npv, n - 1)
                    V.tensor_copy(napt[n % 2][:, 0:nk, :].rearrange("p b n -> p (b n)"),
                                  PS[:, 2 + n % 2, 0:nk * 128]).then_inc(s_npt, 1)

                def na_out(qb):
                    dve.wait_ge(s_npv, 8 * qb + 8)
                    V.reciprocal(rsum[:, 0, 8 * qb:8 * qb + 8], sums[:, 0, 8 * qb:8 * qb + 8])
                    dve.drain()
                    V.tensor_tensor(nao[:, qb, :].rearrange("p (h d) -> p h d", h=HEADS),
                                    PS[:, 4 + qb % 2, :].rearrange("p (h d) -> p h d", h=HEADS),
                                    rsum[:, 0, 8 * qb:8 * qb + 8].unsqueeze(2).broadcast_to([128, HEADS, 64]),
                                    ALU.mult).then_inc(s_no, 1)

                def na_queries(u):
                    V.tensor_tensor(nqz[u % 2][:, :, :],
                                    naq[:, u % 4, u // 4 * 128:u // 4 * 128 + 128].unsqueeze(1).broadcast_to([128, 2, 128]),
                                    wcol[:, W_H0:W_H0 + 2].unsqueeze(2).broadcast_to([128, 2, 128]),
                                    ALU.mult).then_inc(s_nqz, 1)

                dve.wait_ge(s_nqe, 4 + 4)
                na_queries(0)
                na_queries(1)
                for n in range(40):
                    na_max(n)
                    if n % 2 == 1 and n // 2 + 2 < 20:
                        na_queries(n // 2 + 2)
                    if n >= 1:
                        na_keep(n - 1)
                    if n >= 8 and n % 8 == 2:
                        na_out(n // 8 - 1)
                na_keep(39)
                na_out(4)
                for qb in range(NT):
                    dve.wait_ge(s_nyhi, qb + 1)
                    cols = slice(qb * 128, (qb + 1) * 128)
                    V.tensor_tensor(yna_lo[:, :, cols], PS[:, 6 + qb % 2, :].rearrange("p (c n) -> p c n", c=KB),
                                    yna_hi[:, :, cols], ALU.subtract).then_inc(s_yna, 1)
                lam4 = rep[:, R_LAM:R_LAM + 128].rearrange("p (a d) -> p a d", a=4)
                for d in range(2):
                    V.tensor_tensor(lamt[:, 32 * d:32 * d + 32], lam4[:, 2 * d, :], lam4[:, 2 * d + 1, :], ALU.mult)
                dve.drain()
                V.tensor_reduce(lamt[:, 64:66], lamt[:, 0:64].rearrange("p (a d) -> p a d", a=2), AX,
                                ALU.add).then_inc(s_lamv, 1)
                dve.wait_ge(s_lame, 1)
                V.scalar_tensor_tensor(lamt[:, 68:69], lamt[:, 67:68], rep[:, R_LI:R_LI + 1], lamt[:, 66:67],
                                       ALU.subtract, ALU.subtract)
                for n in range(8):
                    dst, r = (daq, daq, daq, daq, dak, dak, dak, dak)[n], draw[n % 2]
                    dve.wait_ge(s_dqe, n + 1 + 4)
                    dve.drain()
                    V.stream_shuffle(dsw[:, :], r[:, C:T], [i ^ 1 for i in range(32)])
                    V.tensor_copy(dst[:, n % 4, 0:C], r[:, 0:C])
                    V.tensor_tensor(dst[:, n % 4, C:T], r[:, C:T], ropec[:, :], ALU.mult)
                    dve.drain()
                    V.tensor_tensor(dsw[:, :], dsw[:, :], ropes[:, :], ALU.mult)
                    dve.drain()
                    V.tensor_tensor(dst[:, n % 4, C:T], dst[:, n % 4, C:T], dsw[:, :], ALU.add).then_inc(s_drope, 1)

                def da_queries(u):
                    V.tensor_tensor(dqz[u % 2][:, :, :],
                                    daq[:, u % 4, u // 4 * 128:u // 4 * 128 + 128].unsqueeze(1).broadcast_to([128, 4, 128]),
                                    wcol[:, W_M0:W_M0 + 4].unsqueeze(2).broadcast_to([128, 4, 128]),
                                    ALU.mult).then_inc(s_dqz, 1)

                def da_max(n):
                    b, q = 3 * (n % 2), 2 * (n % 2)
                    for m, (lo, hi) in enumerate(DA_SPANS[n >= HEADS]):
                        dve.wait_ge(s_ds, 2 * n + m + 1)
                        V.tensor_reduce(mx[:, q + m:q + m + 1], PSF[:, 512 * b + lo:512 * b + hi], AX, ALU.max)
                    dve.drain()
                    V.tensor_scalar(nmx[:, q:q + 2], mx[:, q:q + 2], -DA_SCALE, None, ALU.mult).then_inc(s_dm, 1)

                def da_diff(n):
                    qb, c = n // HEADS, coef[:, n % 2:n % 2 + 1]
                    dve.wait_ge(s_dp, n + 1)
                    V.reciprocal(rsum2[:, 2 * n:2 * n + 2], sum2[:, 2 * n:2 * n + 2])
                    dve.drain()
                    V.scalar_tensor_tensor(c, sum2[:, 2 * n:2 * n + 1], rsum2[:, 2 * n + 1:2 * n + 2],
                                           lamt[:, 68:69], ALU.mult, ALU.mult)
                    dve.drain()
                    p1, p2 = dp1[n % 2], dp2[n % 2]
                    if qb:
                        V.scalar_tensor_tensor(p1[:, 0:512], p2[:, 128:640], c, p1[:, 0:512], ALU.mult, ALU.add)
                    V.scalar_tensor_tensor(p1[:, 512:640], p2[:, 0:128], c, p1[:, 512:640],
                                           ALU.mult, ALU.add).then_inc(s_da, 1)

                def da_out(n):
                    qb, h = n // HEADS, n % HEADS
                    dve.wait_ge(s_dpv, n + 1)
                    V.tensor_scalar(dao[:, qb, 64 * h:64 * h + 64], PS[:, 7, 128:192],
                                    rsum2[:, 2 * n:2 * n + 1], None, ALU.mult).then_inc(s_do, 1)

                dve.drain()
                da_queries(0)
                da_queries(1)
                da_max(0)
                da_max(1)
                da_queries(2)
                for n in range(40):
                    da_diff(n)
                    if n >= 1:
                        da_out(n - 1)
                    if n + 2 < 40:
                        da_max(n + 2)
                    if n % 2 == 1 and (n + 5) // 2 < 20:
                        da_queries((n + 5) // 2)
                da_out(39)
                dve.drain()
                V.tensor_tensor(dosq[:, :, :], dao[:, :, :], dao[:, :, :], ALU.mult)
                dve.drain()
                V.tensor_reduce(ssq[:, :], dosq[:, :, :].rearrange("p t (h d) -> p (t h) d", h=HEADS), AX,
                                ALU.add).then_inc(s_dss, 1)
                dve.wait_ge(s_dsr, 1)
                V.reciprocal(ssq[:, :], ssq[:, :])
                V.tensor_scalar(lamt[:, 0:64], rep[:, R_SUB:R_SUB + 64], rep[:, R_LI + 1:R_LI + 2], None, ALU.mult)
                dve.drain()
                o3 = dao[:, :, :].rearrange("p t (h d) -> p (t h) d", h=HEADS)
                V.tensor_tensor(o3, o3, ssq[:, :].unsqueeze(2).broadcast_to([128, 40, 64]), ALU.mult)
                dve.drain()
                V.tensor_tensor(o3, o3, lamt[:, 0:64].unsqueeze(1).broadcast_to([128, 40, 64]),
                                ALU.mult).then_inc(s_don, 1)
                for qb in range(NT):
                    dve.wait_ge(s_dyhi, qb + 1)
                    cols = slice(qb * 128, (qb + 1) * 128)
                    V.tensor_tensor(yda_lo[:, :, cols], PS[:, qb % 2, :].rearrange("p (c n) -> p c n", c=KB),
                                    yda_hi[:, :, cols], ALU.subtract).then_inc(s_yda, 1)
                with dve.Fori(0, 4) as i:
                    for b in range(3):
                        for m in range(2):
                            g = i * 6 + b * 2 + m
                            if b == 0:
                                dve.drain()
                            dve.wait_ge(s_lift, g + 1)
                            dve.wait_ge(s_sig, g + 1 + 2)
                            if b == 0:
                                ins = V.tensor_tensor(halves(macc[m][:, :]), halves(sig[m][:, :]), pair(m), ALU.mult)
                            else:
                                ins = V.tensor_tensor(halves(sig[m][:, :]), halves(sig[m][:, :]), pair(m), ALU.mult)
                                dve.drain()
                                ins = V.tensor_tensor(macc[m][:, :], macc[m][:, :], sig[m][:, :], ALU.add)
                            ins.then_inc(s_lused, 1)
                            if b == 2:
                                dve.drain().then_inc(s_macc, 1)
                    for m in range(2):
                        dve.wait_ge(s_mhi, i * 2 + m + 1)
                        V.tensor_tensor(mglo[:, 2 * i + m, :], macc[m][:, :], mghi[:, 2 * i + m, :],
                                        ALU.subtract).then_inc(s_mg, 1)

                def add_to_x(m, p, gate, done):
                    p0, p1 = PS[:, 2 * p, :], PS[:, 2 * p + 1, :]
                    for src, cols, sgm in ((p0[:, 0:C], slice(0, C), 0), (p0[:, C:HALF], slice(C, HALF), 1),
                                           (p1[:, 0:HALF], slice(HALF, T), 1)):
                        ins = V.scalar_tensor_tensor(x[:, m, cols], src, mod[:, gate + m, sgm:sgm + 1],
                                                     x[:, m, cols], ALU.mult, ALU.add)
                    ins.then_inc(done, 1)

                for m in range(KD):
                    dve.wait_ge(s_o, m + 1)
                    add_to_x(m, m % 4, 16, s_x)
                dve.drain()
                norm_apply(8, 2)
                for f in range(2):
                    def ffn_mul(i, j):
                        c = f * KFH + i * 2 + j
                        dve.drain()
                        dve.wait_ge(s_silu, c + 1)
                        V.tensor_tensor(halves(gact[j][:, :]), halves(silu[j][:, :]), pair(2 * j + 1),
                                        ALU.mult).then_inc(s_gact, 1)
                        dve.wait_ge(s_ahi, c + 1)
                        V.tensor_tensor(alo[:, i * 2 + j, :], gact[j][:, :], ahi[:, i * 2 + j, :],
                                        ALU.subtract).then_inc(s_act, 1)

                    with dve.Fori(0, KFH // 2) as i:
                        for j in range(2):
                            ffn_mul(i, j)
                    ffn_mul(KFH // 2, 0)
                    if f == 0:
                        dve.wait_ge(s_cond, 32)
                        for n in range(N_ADA - N_ADA2):
                            ada_dot(2, n, N_ADA2 + n)
                        dve.drain()
                        modulation(N_ADA2, N_ADA, mraw[:, 2 * N_ADA2:2 * N_ADA])
                    for m in range(KD):
                        dve.wait_ge(s_f, f * 8 + m + 1)
                        add_to_x(m, m % 4, 40, s_xf)
                end_layer(dve, lay, clears=True)
            dve.wait_ge(s_rt, 1)
            V.reciprocal(rstd[:, :], rstd[:, :])
            dve.drain()
            for k in range(KD):
                V.scalar_tensor_tensor(xo[:, k, :], x[:, k, :], nfin[:, k:k + 1], rstd[:, :],
                                       ALU.mult, ALU.mult).then_inc(s_xo, 1)
            for n in range(2 * NT):
                i, g = n // 2, n % 2
                dve.wait_ge(s_yT, n + 1)
                V.tensor_copy(yo[:, i, g * 512:(g + 1) * 512], PS[:, 2 + n % 6, :]).then_inc(s_yo, 1)

        @block.sync
        def _(sp):
            for n in range(2 * NT):
                i, g = n // 2, n % 2
                sp.wait_ge(s_yo, n + 1)
                sp.dma_start(a["y"][:, i, g * 512:(g + 1) * 512], yo[:, i, g * 512:(g + 1) * 512]).then_inc(s_out, 16)
            sp.wait_ge(s_out, 16 * 10)


SPECTRA = [("A", 0), ("B", 0), ("alt", 0), ("A", 1), ("B", 1), ("alt", 1),
           ("A", 2), ("B", 2), ("A", 3), ("B", 3), ("A", 4), ("B", 4)]
FC_ORDER = [1, 2, 3, 4, 0]
MAGIC = 1.5 * 2.0 ** 23


def _two_pi_parts():
    rest, parts = 2 * math.pi, []
    for bits in (10, 10):
        scale = 2.0 ** (bits - math.ceil(math.log2(rest)))
        part = math.floor(rest * scale) / scale
        parts.append(part)
        rest -= part
    return parts + [float(np.float32(rest))]


TWO_PI = _two_pi_parts()
PI_BELOW = float(np.nextafter(np.float32(math.pi), np.float32(0)))


def grid_rows(src):
    return bass.AP(src.tensor, src.offset, [list(src.ap[0]), [31, ROWS], [1, BLK]])


TOKENS = np.arange(L).reshape(ROWS, 4, BLK).transpose(1, 0, 2).reshape(-1)


def constants():
    f = np.float32
    n = {}
    n["ident"] = np.eye(128, dtype=f)
    n["ones"] = np.ones((128, 128), f)

    def tables(size):
        k = np.arange(size)
        ang = np.pi * ((k[:, None] * k[None, :]) % (2 * size)) / size
        cos, sin = np.cos(ang).astype(f), np.sin(ang).astype(f)
        fwd, inv = sin.copy(), sin.copy()
        fwd[:, 0] = inv[0, :] = 1 - 2 * (k % 2)
        return cos, fwd, inv

    for name, m in zip(("ctab", "stab", "sinv"), tables(L)):
        n[name] = np.ascontiguousarray(m.reshape(4, 128, L).transpose(1, 0, 2))
    for name, m in zip(("cctab", "cstab", "csinv"), tables(C)):
        n[name] = m
    feats, decays = [], []
    for size in (C, L):
        pos = np.arange(size, dtype=f)
        t = pos / f(size)
        bands = np.linspace(1e-4, 15, 16).astype(f)
        ang = f(2 * math.pi / size) * pos[:, None] * bands[None, :]
        feats.append(np.concatenate([t[:, None], np.cos(ang), -np.sin(ang)], axis=-1).astype(f))
        deltas = np.linspace(math.log(1e-2) / 1.5, math.log(1e-2) / 0.3, BW).astype(f)
        decays.append(np.exp(-t[:, None] * np.abs(deltas)[None, :]).astype(f))
    n["feats"] = np.ascontiguousarray(np.concatenate(feats).T)
    n["decay"] = np.ascontiguousarray(np.concatenate(decays).reshape(NT, 128, BW).transpose(1, 0, 2))
    wc = np.zeros((128, W_END), f)
    for col, size in ((W_LA, L), (W_CA, C)):
        wc[:, col] = wc[:, col + 1] = 1.0 / size
        wc[0, col], wc[0, col + 1] = 0.5 / size, 0.0
    wc[:, W_EPS] = EPS
    for m in range(4):
        wc[:, W_M0 + m] = np.arange(128) // 32 == m
    for m in range(2):
        wc[:, W_H0 + m] = np.arange(128) // 64 == m
    n["wcol"] = wc
    pos = np.arange(L)[TOKENS]
    inv = (10000.0 ** (-np.arange(8, dtype=f) / 8)).astype(f)
    ang = np.concatenate([(pos // GW).astype(f)[:, None] * inv, (pos % GW).astype(f)[:, None] * inv], axis=-1)
    p = np.arange(128)
    n["ropec"] = np.ascontiguousarray(np.cos(ang).astype(f)[:, (p % 32) // 2].T)
    sign = np.where(p % 2 == 0, -1.0, 1.0).astype(f)
    n["ropes"] = np.ascontiguousarray((np.sin(ang).astype(f)[:, (p % 32) // 2] * sign).T)
    col = lambda b: BLK * b + np.arange(128) % BLK
    mask = np.zeros((128, 10, 128), f)
    for j, blocks in enumerate(NA_BLOCKS):
        cq = col(j)
        c0 = np.clip(cq - BLK // 2, 0, GW - BLK)
        for r, b in enumerate(blocks):
            ck = col(b)
            ok = (ck[None, :] >= c0[:, None]) & (ck[None, :] < c0[:, None] + BLK)
            mask[:, MASK0[j] + r, :] = np.where(ok, 0.0, NEG)
    n["maskb"] = mask
    li = [0.8 - 0.6 * math.exp(-0.3 * l) for l in range(DEPTH)]
    return n, li


def kernel(**inputs):
    import ml_dtypes
    import concourse.bacc as bacc
    from concourse import mybir as mb
    from concourse.bass_utils import run_bass_kernel_spmd

    g = {k: np.asarray(v) for k, v in inputs.items()}
    n, li = constants()
    for name in ("maskb",):
        n[name] = n[name].astype(ml_dtypes.bfloat16)
    n["identb"] = n["ident"].astype(ml_dtypes.bfloat16)

    def chunks(v):
        v = v.reshape(v.shape[:-1] + (-1, 128))
        return np.moveaxis(v, -1, 0).reshape(128, -1)

    def cols(w, c0, k=KD):
        return w[:, c0:c0 + 128].reshape(k, 128, 128).transpose(1, 0, 2).reshape(128, -1)

    strips, adas = [], []
    for l in range(DEPTH):
        wi, wl, wo, wf, wg = (g[k][l] for k in ("w_in", "w_lift", "w_out", "w_ffn_in", "w_ffn_out"))
        adas += [g["w_ada"][l][:, 128 * m:128 * m + 128].T for m in range(N_ADA)]
        strips += [cols(wi, 128 * m) for m in range(12)]
        for b in (1536, 3072):
            strips += [cols(wi, b + 128 * m) for m in range(8)]
            for s in range(4):
                v = wi[256 * s:256 * s + 256, b + 1024:b + 1536].reshape(2, 128, 512)
                strips.append(v.transpose(1, 0, 2).reshape(128, -1))
        for mp in range(4):
            for b in range(3):
                strips += [cols(wi, 4608 + b * D + 128 * (2 * mp + m)) for m in range(2)]
                strips.append(np.concatenate([cols(wl[b], 128 * (2 * mp + m), KB) for m in range(2)], axis=1))
        strips += [cols(wo, 128 * m) for m in range(8)]
        for f in range(2):
            for j in range(KFH):
                c0 = 128 * (f * KFH + j)
                strips += [cols(wf, c0), cols(wf, DFF + c0)]
            rows = wg[f * KFH * 128:(f + 1) * KFH * 128].reshape(KFH, 128, KD, 128)
            tiles = rows.transpose(2, 0, 1, 3).reshape(N_FOUT, KD, 128, 128)
            strips += [t.transpose(1, 0, 2).reshape(128, -1) for t in tiles]
    n["w_strips"] = np.stack(strips)
    n["w_ada"] = np.stack(adas).reshape(DEPTH, N_ADA, 128, D)
    tok = np.concatenate([g["x_prompt"][0], g["x_sample"][0][TOKENS]])
    n["x_in"] = tok.reshape(NT, 128, D).transpose(1, 0, 2)
    n["cond"] = np.broadcast_to(np.stack([g["c_ctx"].reshape(-1), g["c"][0].reshape(-1)]), (128, 2, D))
    n["nfin"] = chunks(g["norm_final"])
    n["par"] = np.stack([np.concatenate([chunks(g[k][l]) for k in (
        "b_ada", "norm_mix", "norm_ffn", "hy_conv_w", "hy_conv_b", "hy_bias")], axis=1) for l in range(DEPTH)])
    n["rep"] = np.stack([np.concatenate([
        np.broadcast_to(v.reshape(1, -1), (128, v.size)) for v in (
            g["da_subln"][l], g["da_lambda"][l], np.array([li[l], 1 - li[l]], np.float32))], axis=1)
        for l in range(DEPTH)])
    n["fw1"], n["fw2"] = g["hy_filt_w1"], g["hy_filt_w2"]
    n["fw3"] = g["hy_filt_w3"].reshape(DEPTH, HID, 4, BW)
    n["fvec"] = np.stack([g["hy_filt_b1"], g["hy_filt_b2"], g["hy_filt_freq"]], -1)
    for k in ("cache_na_k", "cache_na_v", "cache_da_k", "cache_da_v"):
        n[k] = g[k][0].reshape(DEPTH, 128, BW)
    flat = g["na_rpb"].reshape(DEPTH, HEADS, 15 * 31)
    flat = np.pad(flat, ((0, 0), (0, 0), (32, 64)))
    p = np.arange(128)
    start = 32 + (7 - p // BLK) * 31 + 15 - p % BLK - BLK
    n["rpb"] = flat[:, :, start[:, None] + np.arange(7 * 31 + 48)[None, :]].transpose(0, 2, 1, 3)

    outs = {"y": (128, NT, D)}
    for k in ("new_na_k", "new_na_v", "new_da_k", "new_da_v"):
        outs[k] = (DEPTH, 128, BW)
    nc = bacc.Bacc("TRN2", target_bir_lowering=False, num_devices=1)
    arrays, aps = {}, {}
    for k, v in n.items():
        v = np.ascontiguousarray(v)
        arrays[f"in_{k}"] = v
        aps[k] = nc.dram_tensor(f"in_{k}", v.shape, mb.dt.from_np(v.dtype), kind="ExternalInput").ap()
    for k, s in outs.items():
        aps[k] = nc.dram_tensor(f"out_{k}", s, mb.dt.float32, kind="ExternalOutput").ap()
    build(nc, aps)
    r = run_bass_kernel_spmd(nc, [arrays], core_ids=[0]).results[0]
    y = np.asarray(r["out_y"]).transpose(1, 0, 2).reshape(T, D)
    ys = y[C:][np.argsort(TOKENS)]
    nak, nav, dak, dav = (np.asarray(r[f"out_{k}"]) for k in ("new_na_k", "new_na_v", "new_da_k", "new_da_v"))
    shape = (1, DEPTH, C, HEADS, 64)
    return (y[None, 0:C], ys[None], nak.reshape(shape), nav.reshape(shape), dak.reshape(shape),
            dav.reshape(shape))
```
